# Optimizing a Trainium2 kernel written in Bass

```python
import jax, jax.numpy as jnp
from jax import lax
import numpy as np

D_MODEL = 1024
BATCH = 1
SEQ = 512
DEPTH = 2

GLA_HEADS = 4
GLA_DK = D_MODEL // 2 // GLA_HEADS
GLA_DV = D_MODEL // GLA_HEADS
GLA_GATE_RANK = 16
GLA_TAU = 16.0
GLA_CHUNK = 64
SWA_HEADS = 16
SWA_KV_HEADS = 2
SWA_HD = 64
WINDOW = 128
SWA_BLOCK = 128
N_BUCKETS = 32
MAX_DISTANCE = 128
PEER_HEADS = 8
PEER_NKEYS = 128
PEER_NEXPERTS = PEER_NKEYS * PEER_NKEYS
PEER_QDIM = 256
PEER_TOPK = 16
PEER_TOKEN_BLOCK = 128
EPS = 1e-6

GLA_QK_W = GLA_HEADS * GLA_DK
GLA_V_W = GLA_HEADS * GLA_DV
SWA_Q_W = SWA_HEADS * SWA_HD
SWA_KV_W = SWA_KV_HEADS * SWA_HD
SPLIT_SIZES = (GLA_QK_W, GLA_QK_W, GLA_V_W, GLA_GATE_RANK, GLA_V_W, SWA_Q_W, SWA_KV_W, SWA_KV_W, D_MODEL, D_MODEL)
IN_W = GLA_QK_W * 2 + GLA_V_W * 2 + GLA_GATE_RANK + SWA_Q_W + SWA_KV_W * 2 + D_MODEL * 2

kernel_name = 'hybrid_gla_swa_peer_block'

def _split_points():
    return [int(s) for s in np.cumsum(SPLIT_SIZES)[:-1]]

def _rms_f32(x, g):
    xf = x.astype(jnp.float32)
    y = xf * lax.rsqrt(jnp.mean(xf * xf, axis=-1, keepdims=True) + EPS)
    return y * g.astype(jnp.float32)

def rms_norm(x, g):
    return _rms_f32(x, g).astype(x.dtype)

def t5_causal_bucket(dist):
    max_exact = N_BUCKETS // 2
    d = np.maximum(dist, 1).astype(np.float32)
    large = max_exact + (np.log(d / max_exact) / np.log(MAX_DISTANCE / max_exact)
                         * (N_BUCKETS - max_exact)).astype(np.int32)
    large = np.minimum(large, N_BUCKETS - 1)
    return np.where(dist < max_exact, dist, large).astype(np.int32)

def gla_branch(q, k, v, gate_lr, r, w2, b2, norm_g):
    B, T, _ = q.shape
    dt = q.dtype
    f32 = jnp.float32
    q = q.reshape(B, T, GLA_HEADS, GLA_DK).astype(f32) * (GLA_DK ** -0.5)
    k = k.reshape(B, T, GLA_HEADS, GLA_DK).astype(f32)
    v = v.reshape(B, T, GLA_HEADS, GLA_DV).astype(f32)
    log_a = jax.nn.log_sigmoid((gate_lr @ w2 + b2).astype(f32)) / GLA_TAU
    log_a = log_a.reshape(B, T, GLA_HEADS, GLA_DK)
    n_chunks = T // GLA_CHUNK

    def to_chunks(a):
        return a.reshape(B, n_chunks, GLA_CHUNK, a.shape[2], a.shape[3]).transpose(1, 0, 2, 3, 4)

    qc, kc, vc, gc = to_chunks(q), to_chunks(k), to_chunks(v), to_chunks(log_a)
    causal = jnp.tril(jnp.ones((GLA_CHUNK, GLA_CHUNK), dtype=bool))

    def step(S, inp):
        qn, kn, vn, gn = inp
        b = jnp.cumsum(gn, axis=1)
        b_last = b[:, -1]
        q_dec = qn * jnp.exp(b)
        k_inv = kn * jnp.exp(-b)
        attn = jnp.where(causal, jnp.einsum('bthd,bshd->bhts', q_dec, k_inv), 0.0)
        o = (jnp.einsum('bhts,bshv->bthv', attn, vn)
             + jnp.einsum('bthd,bhdv->bthv', q_dec, S))
        k_tail = kn * jnp.exp(b_last[:, None] - b)
        S = S * jnp.exp(b_last)[..., None] + jnp.einsum('bshd,bshv->bhdv', k_tail, vn)
        return S, o

    S0 = jnp.zeros((B, GLA_HEADS, GLA_DK, GLA_DV), f32)
    _, o = lax.scan(step, S0, (qc, kc, vc, gc))
    o = o.transpose(1, 0, 2, 3, 4).reshape(B, T, GLA_HEADS, GLA_DV)
    o = _rms_f32(o, norm_g).reshape(B, T, GLA_V_W)
    o = o * jax.nn.silu(r.astype(f32))
    return o.astype(dt)

def swa_branch(q, k, v, qn_g, kn_g, sinks, rel_bias):
    B, T, _ = q.shape
    dt = q.dtype
    f32 = jnp.float32
    G = SWA_HEADS // SWA_KV_HEADS
    BLK = SWA_BLOCK
    NB = T // BLK
    q = _rms_f32(q.reshape(B, T, SWA_KV_HEADS, G, SWA_HD), qn_g) * (SWA_HD ** -0.5)
    k = _rms_f32(k.reshape(B, T, SWA_KV_HEADS, SWA_HD), kn_g)
    v = v.reshape(B, T, SWA_KV_HEADS, SWA_HD).astype(f32)

    pad = jnp.zeros((B, BLK, SWA_KV_HEADS, SWA_HD), f32)

    def windows(a):
        ap = jnp.concatenate([pad, a], axis=1).reshape(B, NB + 1, BLK, SWA_KV_HEADS, SWA_HD)
        w = jnp.concatenate([ap[:, :-1], ap[:, 1:]], axis=2)
        return w.transpose(1, 0, 2, 3, 4)

    kw, vw = windows(k), windows(v)
    qb = q.reshape(B, NB, BLK, SWA_KV_HEADS, G, SWA_HD).transpose(1, 0, 2, 3, 4, 5)

    qi = np.arange(BLK)[:, None]
    sj = np.arange(2 * BLK)[None, :]
    dist = BLK + qi - sj
    band = (dist >= 0) & (dist < WINDOW)
    key_pos = np.arange(NB)[:, None, None] * BLK + sj[None] - BLK
    valid = jnp.asarray(band[None] & (key_pos >= 0))
    bucket = t5_causal_bucket(np.clip(dist, 0, None))
    bias = rel_bias[bucket].astype(f32)
    bias = bias.transpose(2, 0, 1).reshape(SWA_KV_HEADS, G, BLK, 2 * BLK)
    sink = sinks.astype(f32).reshape(SWA_KV_HEADS, G, 1, 1)

    def block(args):
        qn, kn, vn, ok = args
        logits = jnp.einsum('bqkgd,bskd->bkgqs', qn, kn) + bias
        logits = jnp.where(ok, logits, -jnp.inf)
        m = jnp.maximum(jnp.max(logits, axis=-1, keepdims=True), sink)
        p = jnp.exp(logits - m)
        denom = jnp.sum(p, axis=-1, keepdims=True) + jnp.exp(sink - m)
        return jnp.einsum('bkgqs,bskd->bqkgd', p / denom, vn)

    out = lax.map(block, (qb, kw, vw, valid))
    out = out.transpose(1, 0, 2, 3, 4, 5).reshape(B, T, SWA_Q_W)
    return out.astype(dt)

def peer_ffn(h, wq, subkeys, u, v):
    B, T, D = h.shape
    dt = h.dtype
    f32 = jnp.float32
    K = PEER_TOPK
    q = (h @ wq).reshape(B, T, PEER_HEADS, 2, PEER_QDIM // 2).astype(f32)
    s = jnp.einsum('bthpd,pnd->bthpn', q, subkeys.astype(f32))
    s_top, i_top = lax.top_k(s, K)
    cand = s_top[..., 0, :, None] + s_top[..., 1, None, :]
    cand_idx = i_top[..., 0, :, None] * PEER_NKEYS + i_top[..., 1, None, :]
    best, pos = lax.top_k(cand.reshape(B, T, PEER_HEADS, K * K), K)
    experts = jnp.take_along_axis(cand_idx.reshape(B, T, PEER_HEADS, K * K), pos, axis=-1)
    gates = jax.nn.softmax(best, axis=-1)

    n_blocks = (B * T) // PEER_TOKEN_BLOCK
    hb = h.reshape(n_blocks, PEER_TOKEN_BLOCK, D)
    eb = experts.reshape(n_blocks, PEER_TOKEN_BLOCK, PEER_HEADS * K)
    gb = gates.reshape(n_blocks, PEER_TOKEN_BLOCK, PEER_HEADS * K).astype(dt)

    def block(args):
        hx, e, g = args
        a = jnp.einsum('td,tkd->tk', hx, u[e])
        return jnp.einsum('tk,tkd->td', g * jax.nn.gelu(a), v[e])

    y = lax.map(block, (hb, eb, gb))
    return y.reshape(B, T, D)

def setup_inputs(seed: int = 0) -> dict:
    key = jax.random.key(seed)
    ks = jax.random.split(key, 21)
    f32 = jnp.float32
    nrm = lambda k, shape, s: jax.random.normal(k, shape, f32) * s
    L, D = DEPTH, D_MODEL
    return {
        'x': nrm(ks[0], (BATCH, SEQ, D), 1.0),
        'c': nrm(ks[1], (BATCH, D), 1.0),
        'w_ada': nrm(ks[2], (L, D, 6 * D), 0.5 * D ** -0.5),
        'b_ada': nrm(ks[3], (L, 6 * D), 0.02),
        'norm1_g': 1.0 + nrm(ks[4], (L, D), 0.02),
        'w_in': nrm(ks[5], (L, D, IN_W), D ** -0.5),
        'gla_gate_w2': nrm(ks[6], (L, GLA_GATE_RANK, GLA_QK_W), GLA_GATE_RANK ** -0.5),
        'gla_gate_b': nrm(ks[7], (L, GLA_QK_W), 0.1),
        'gla_norm_g': 1.0 + nrm(ks[8], (L, GLA_DV), 0.02),
        'swa_qnorm_g': 1.0 + nrm(ks[9], (L, SWA_HD), 0.02),
        'swa_knorm_g': 1.0 + nrm(ks[10], (L, SWA_HD), 0.02),
        'swa_sinks': nrm(ks[11], (L, SWA_HEADS), 0.5),
        'rel_bias': nrm(ks[12], (N_BUCKETS, SWA_HEADS), 0.2),
        'w_up_a': nrm(ks[13], (L, GLA_V_W, D), GLA_V_W ** -0.5),
        'w_up_b': nrm(ks[14], (L, SWA_Q_W, D), SWA_Q_W ** -0.5),
        'w_out': nrm(ks[15], (L, D, D), D ** -0.5),
        'norm2_g': 1.0 + nrm(ks[16], (L, D), 0.02),
        'peer_wq': nrm(ks[17], (L, D, PEER_HEADS * PEER_QDIM), D ** -0.5),
        'peer_subkeys': nrm(ks[18], (L, 2, PEER_NKEYS, PEER_QDIM // 2), (PEER_QDIM // 2) ** -0.5),
        'peer_u': nrm(ks[19], (L, PEER_NEXPERTS, D), D ** -0.5),
        'peer_v': nrm(ks[20], (L, PEER_NEXPERTS, D), 1.0),
    }

def reference(x, c, w_ada, b_ada, norm1_g, w_in, gla_gate_w2, gla_gate_b, gla_norm_g,
              swa_qnorm_g, swa_knorm_g, swa_sinks, rel_bias, w_up_a, w_up_b, w_out,
              norm2_g, peer_wq, peer_subkeys, peer_u, peer_v):
    splits = _split_points()
    for l in range(DEPTH):
        mod = jax.nn.silu(c) @ w_ada[l] + b_ada[l]
        sh1, sc1, g1, sh2, sc2, g2 = jnp.split(mod, 6, axis=-1)

        h = rms_norm(x, norm1_g[l]) * (1.0 + sc1[:, None]) + sh1[:, None]
        proj = h @ w_in[l]
        gq, gk, gv, glr, gr, sq, sk, sv, ga, gb = jnp.split(proj, splits, axis=-1)
        ya = gla_branch(gq, gk, gv, glr, gr, gla_gate_w2[l], gla_gate_b[l], gla_norm_g[l]) @ w_up_a[l]
        yb = swa_branch(sq, sk, sv, swa_qnorm_g[l], swa_knorm_g[l], swa_sinks[l], rel_bias) @ w_up_b[l]
        mixed = (jax.nn.sigmoid(ga) * ya + jax.nn.sigmoid(gb) * yb) @ w_out[l]
        x = x + g1[:, None] * mixed

        h2 = rms_norm(x, norm2_g[l]) * (1.0 + sc2[:, None]) + sh2[:, None]
        x = x + g2[:, None] * peer_ffn(h2, peer_wq[l], peer_subkeys[l], peer_u[l], peer_v[l])
    return x


_drawn_inputs = setup_inputs


def setup_inputs(seed=0):
    import zlib

    import numpy as np

    out = dict(_drawn_inputs(seed))
    spreads = {}
    factors = {'gla_norm_g': 3.495, 'swa_qnorm_g': 7.51, 'swa_knorm_g': 6.515, 'swa_sinks': 53.692}
    for name, (base, spread) in spreads.items():
        noise = np.random.default_rng([zlib.crc32(name.encode()), seed]).standard_normal(out[name].shape)
        drawn = base * np.exp(spread * noise) if base else spread * noise
        out[name] = __import__('jax').numpy.asarray(drawn.astype(out[name].dtype))
    for name, factor in factors.items():
        out[name] = (out[name] * factor).astype(out[name].dtype)
    return out
```

```python
from contextlib import ExitStack

import numpy as np

import concourse.bass as bass
from concourse import mybir

ALU = mybir.AluOpType
ACT = mybir.ActivationFunctionType
F32 = mybir.dt.float32
F32R = mybir.dt.float32r
U32 = mybir.dt.uint32
AX_X = mybir.AxisListType.X

P = 128
DEPTH, SEQ, D = 2, 512, 1024
TT = SEQ // P
KC = D // P
GH, DK, DV, CHUNK = 4, 128, 256, 64
SH, HD = 16, 64
EPS = 1e-6
NEG = -1.0e30
LOWEST = -3.0e38
GLA_TAU = 16.0
PH, NK, TOPK = 8, 128, 16
PICKS = PH * TOPK
GT = 64

N_ADA = 6 * KC
U_Q, U_K, U_LR, U_V, U_SQ, U_SK, U_SV, U_R, U_MIX = 0, 4, 8, 9, 17, 25, 27, 28, 36
U_OUT, U_WQ, U_U = 68, 76, 92
U_VE = U_U + NK
N_SPLIT = U_VE + NK
N_STREAM = N_ADA + N_SPLIT
RAW = 4
ROUNDS = N_STREAM // RAW

COLUMN_UNITS = ([(m, "act") for m in range(0, 9)] + [(m, "act") for m in range(17, 28)]
                + [(m, "act" if (m - U_MIX) % 2 == 0 else "dve") for m in range(U_MIX, U_OUT)]
                + [(m, "dve") for m in range(U_WQ, U_U)] + [(m, "act") for m in range(U_U, U_VE)])
ORDER = {m: n for n, (m, _) in enumerate(COLUMN_UNITS)}
DONE = {}
for _m, _e in COLUMN_UNITS:
    DONE[_m] = (_e, sum(1 for k, e in COLUMN_UNITS if e == _e and k <= _m))
ACT_DONE = sum(1 for _, e in COLUMN_UNITS if e == "act")
DVE_DONE = sum(1 for _, e in COLUMN_UNITS if e == "dve")

C_IDENT, C_IOTA, C_SCAN, C_CAUSAL, C_HEADS, C_ONES, N_CONST = 0, 128, 256, 768, 896, 1024, 1152
V_N1, V_N2, V_BADA, V_GB, V_QN, V_KN, N_COLS = 0, 8, 16, 64, 68, 69, 70


def constants():
    c = np.zeros((P, N_CONST), np.float32)
    i = np.arange(P)
    c[:, C_IDENT:C_IDENT + P] = np.eye(P)
    c[:, C_IOTA:C_IOTA + P] = i[None, :]
    c[:, C_SCAN:C_SCAN + SEQ] = (np.arange(SEQ) % CHUNK != 0)[None, :]
    same = i[:, None] // CHUNK == i[None, :] // CHUNK
    c[:, C_CAUSAL:C_CAUSAL + P] = same & (i[:, None] <= i[None, :])
    c[:, C_HEADS:C_HEADS + P] = (i[:, None] // HD == i[None, :] // HD) / HD
    c[:, C_ONES:C_ONES + P] = 1.0
    return c


def band_mask():
    dist = 255 - np.arange(384)
    return np.broadcast_to(np.where((dist >= 0) & (dist < 128), 0.0, NEG), (P, 384)).astype(np.float32)


def bucket_onehot():
    dist = 255 - np.arange(384)
    d = np.maximum(dist, 1).astype(np.float32)
    large = 16 + (np.log(d / 16) / np.log(128 / 16) * 16).astype(np.int32)
    bucket = np.where(dist < 16, dist, np.minimum(large, 31))
    out = np.zeros((32, 384), np.float32)
    for k in range(384):
        if 0 <= dist[k] < 128:
            out[bucket[k], k] = 1.0
    return out


class Chain:

    def __init__(self, eng, sem):
        self.eng, self.sem, self.n, self.off = eng, sem, 0, 0

    def __call__(self, ins):
        self.n += 1
        ins.then_inc(self.sem, 1)
        self.eng.wait_ge(self.sem, self.off + self.n)

    def enter(self, i, per):
        self.saved, self.per = self.n, per
        self.off, self.n = i * per + self.saved, 0

    def leave(self, count):
        assert self.n == self.per, self.n
        self.off, self.n = 0, self.saved + count * self.per


def trunk(nc, stream, x_in, c_in, cols_in, rows_in, w2_in, sub_in, rel_in, onehot_in, mask_in, const_in,
          out):
    band_d = nc.dram_tensor("band_bias", (SH, P * 384), F32, kind="Internal").ap()
    act_d = nc.dram_tensor("expert_act", (NK, P, SEQ), F32, kind="Internal").ap()
    gate_d = nc.dram_tensor("expert_gate", (SEQ // GT, P, NK, GT), F32, kind="Internal").ap()
    base = (nc.sbuf_base + 31) // 32 * 32

    def at(name, kb, shape, dt=F32):
        return nc.alloc_sbuf_tensor_at(name, shape, dt, offset=base + int(kb * 1024))

    x = at("x", 0, [P, TT, D])
    raw = at("raw", 16, [P, RAW, 1024])
    w_hi = at("w_hi", 32, [P, 2, 1024], F32R)
    w_lo = at("w_lo", 40, [P, 2, 1024], F32R)
    h_hi = at("h_hi", 48, [P, KC, SEQ], F32R)
    h_lo = at("h_lo", 64, [P, KC, SEQ], F32R)
    const = at("const", 80, [P, N_CONST])
    grow = at("grow", 84.5, [P, 2, D])
    cols = at("cols", 92.5, [P, N_COLS])
    rows = at("rows", 92.8125, [P, DV + SH])
    mod = at("mod", 93.875, [P, N_ADA])
    small = at("small", 94.0625, [P, 112])
    silu_c = at("silu_c", 94.5, [P, KC])
    Z = 94.5625
    v_g = at("v_g", Z + 0, [P, TT, D])
    r_g = at("r_g", Z + 16, [P, TT, D])
    qT_s = at("qT_s", Z + 32, [P, 8, SEQ])
    kT_s = at("kT_s", Z + 48, [P, 2, SEQ])
    vT_s = at("vT_s", Z + 52, [P, SEQ])
    v_s = at("v_s", Z + 54, [P, TT, P])
    q_g = at("q_g", Z + 56, [P, GH, SEQ])
    k_g = at("k_g", Z + 64, [P, GH, SEQ])
    kinv = at("kinv", Z + 72, [P, GH, SEQ])
    ktail = at("ktail", Z + 80, [P, GH, TT, P])
    tmp = at("tmp", Z + 88, [P, 5, SEQ])
    attnT = at("attnT", Z + 98, [P, 2, GH, P])
    state = at("state", Z + 102, [P, 2, GH, DV])
    w2 = at("w2", Z + 102, [16, SEQ])
    lrT = at("lrT", Z + 110, [16, SEQ])
    xn = at("xn", Z + 16, [P, TT, D])
    junk = at("junk", Z + 0, [P, D])
    hf = at("hf", Z + 88, [P, 2, SEQ])
    oa_hi = at("oa_hi", Z + 56, [P, KC, SEQ], F32R)
    oa_lo = at("oa_lo", Z + 72, [P, KC, SEQ], F32R)
    o_s = at("o_s", Z + 0, [P, TT, D])
    logit = at("logit", Z + 16, [P, 2, TT, 256])
    pT = at("pT", Z + 24, [P, 2, 8, P])
    bias_s = at("bias_s", Z + 88, [P, SH, 256])
    ob_hi = at("ob_hi", Z + 16, [P, KC, SEQ], F32R)
    ob_lo = at("ob_lo", Z + 88, [P, KC, SEQ], F32R)
    mixedT = at("mixedT", Z + 32, [P, KC, SEQ])
    sig = at("sig", Z + 0, [P, 4, SEQ])
    part = at("part", Z + 8, [P, 2, SEQ])
    diag = at("diag", Z + 88, [P, 16, P])
    xadd = at("xadd", Z + 0, [P, TT, SEQ])
    scores = at("scores", Z + 0, [P, TT, 16, P])
    gel = at("gel", Z + 32, [P, 2, SEQ])
    q_hi = at("q_hi", Z + 36, [P, 2, SEQ], F32R)
    q_lo = at("q_lo", Z + 40, [P, 2, SEQ], F32R)
    sub_raw = at("sub_raw", Z + 44, [P, 256])
    sub_hi = at("sub_hi", Z + 45, [P, 256], F32R)
    sub_lo = at("sub_lo", Z + 46, [P, 256], F32R)
    top = at("top", Z + 48, [P, TT, 16, TOPK])
    topi = at("topi", Z + 52, [P, TT, 16, TOPK], U32)
    topf = at("topf", Z + 56, [P, TT, 16, TOPK])
    rest = at("rest", Z + 60, [P, TT, 256])
    cand = at("cand", Z + 64, [P, TT, 256])
    best = at("best", Z + 68, [P, TT, PH, TOPK])
    posi = at("posi", Z + 70, [P, TT, PH, TOPK], U32)
    half_i = at("half_i", Z + 72, [P, PICKS], U32)
    half_f = at("half_f", Z + 72.5, [P, PICKS])
    picked = at("picked", Z + 73, [P, 3, PICKS])
    gden = at("gden", Z + 74.5, [P, 16])
    match = at("match", Z + 76, [P, PH * TOPK, TOPK])
    pair_s = at("pair_s", Z + 84, [P, TT, 2, P])
    pair_t = at("pair_t", Z + 88, [P, TT, 2, TOPK])
    pair_i = at("pair_i", Z + 88.5, [P, TT, 2, TOPK], U32)
    pair_r = at("pair_r", Z + 89, [P, TT, 2, P])
    g_round = at("g_round", Z + 14, [P, TT, P], F32R)
    idxT = at("idxT", Z + 100, [P, TT, 4, P])
    gatebuf = at("gatebuf", Z + 36, [P, 2, NK, GT])
    hot_j = at("hot_j", Z + 0, [P, 2, 4, P], F32R)
    hot_i = at("hot_i", Z + 4, [P, 2, 4, 2, P], F32R)
    pick = at("pick", Z + 12, [P, 4, P])
    y = at("y", Z + 0, [P, TT, D])
    g_hi = at("g_hi", Z + 16, [P, 2, 8, SEQ], F32R)
    g_lo = at("g_lo", Z + 48, [P, 2, 8, SEQ], F32R)
    a_in = at("a_in", Z + 80, [P, 4, 2, SEQ])
    g_in = at("g_in", Z + 96, [P, 4, SEQ // GT, 2, GT])
    rel = at("rel", Z + 0, [32, SH])
    onehot = at("onehot", Z + 1, [32, 384])
    rel_b = at("rel_b", Z + 4, [32, SH, P])
    mask_s = at("mask_s", Z + 2.5, [P, 384])
    band = at("band", Z + 56, [P, SH, 384])

    ident = const[:, C_IDENT:C_IDENT + P]
    iota = const[:, C_IOTA:C_IOTA + P]

    with ExitStack() as ctx:
        ps = ctx.enter_context(nc.psum_tensor("ps", [P, 8, 512], F32))

        def sem(name):
            return ctx.enter_context(nc.semaphore(name))

        raw_loaded = [sem(f"raw_loaded{b}") for b in range(RAW)]
        ada_used, hi_ready, lo_ready, unit_used = sem("ada_used"), sem("hi_ready"), sem("lo_ready"), sem("unit_used")
        col_act, col_dve, row_done = sem("col_act"), sem("col_dve"), sem("row_done")
        consts_loaded, x_loaded, params_loaded, small_free = (sem("consts_loaded"), sem("x_loaded"),
                                                              sem("params_loaded"), sem("small_free"))
        rel_rep, band_mm, band_out, band_stored, bias_loaded, bias_free = (
            sem("rel_rep"), sem("band_mm"), sem("band_out"), sem("band_stored"), sem("bias_loaded"), sem("bias_free"))
        silu_ready, mod_ready, diag_ready, grow_mm = sem("silu_ready"), sem("mod_ready"), sem("diag_ready"), sem("grow_mm")
        sumsq, meansq, rstd, xn_ready, xT_mm, hf_ready, hhi_ready, h_ready = (
            sem("sumsq"), sem("meansq"), sem("rstd"), sem("xn_ready"), sem("xT_mm"), sem("hf_ready"),
            sem("hhi_ready"), sem("h_ready"))
        x_ready = sem("x_ready")
        silu_r, gate_mm, soft, decay, decay_exp, keys_ready, tail_mm, tail_ready = (
            sem("silu_r"), sem("gate_mm"), sem("soft"), sem("decay"), sem("decay_exp"),
            sem("keys_ready"), sem("tail_mm"), sem("tail_ready"))
        attn_mm, attn_ready, upd_mm, state_ready, o_mm, o_sq, o_ms, o_rstd, o_done = (
            sem("attn_mm"), sem("attn_ready"), sem("upd_mm"), sem("state_ready"), sem("o_mm"), sem("o_sq"),
            sem("o_ms"), sem("o_rstd"), sem("o_done"))
        tr_mm, tr_hi, tr_done = sem("tr_mm"), sem("tr_hi"), sem("tr_done")
        sq_ready, sq_mm, sq_inv, sq_root, sqk_ready, vs_mm, vs_ready = (
            sem("sq_ready"), sem("sq_mm"), sem("sq_inv"), sem("sq_root"), sem("sqk_ready"), sem("vs_mm"), sem("vs_ready"))
        logit_mm, logit_ready, prob_ready, pT_mm, pT_ready, os_mm, os_ready = (
            sem("logit_mm"), sem("logit_ready"), sem("prob_ready"), sem("pT_mm"), sem("pT_ready"), sem("os_mm"),
            sem("os_ready"))
        mixed_sum, mixed_hi, mixed_ready, row_dve = sem("mixed_sum"), sem("mixed_hi"), sem("mixed_ready"), sem("row_dve")
        sub_loaded, subhi_ready, sub_ready, qhi_ready, score_mm, score_ready = (
            sem("sub_loaded"), sem("subhi_ready"), sem("sub_ready"), sem("qhi_ready"), sem("score_mm"), sem("score_ready"))
        gexp_in, gexp, picked_ready, pick_mm, ghi_ready, idx_ready = (
            sem("gexp_in"), sem("gexp"), sem("picked_ready"), sem("pick_mm"), sem("ghi_ready"), sem("idx_ready"))
        hot_ready, hot_used, gate_ready, gate_stored = (sem("hot_ready"), sem("hot_used"), sem("gate_ready"),
                                                        [sem("gate_stored0"), sem("gate_stored1")])
        gel_ready, gel_stored = sem("gel_ready"), [sem("gel_stored0"), sem("gel_stored1")]
        ag_loaded, w_prod, w_hi_ready, w_ready = ([sem(f"ag_loaded{b}") for b in range(4)], sem("w_prod"),
                                                  sem("w_hi_ready"), sem("w_ready"))
        y_done, out_ready, out_stored = sem("y_done"), sem("out_ready"), sem("out_stored")
        act_step, dve_step, fence = sem("act_step"), sem("dve_step"), sem("fence")
        y_zero = sem("y_zero")

        block = ctx.enter_context(nc.Block())

        def used(l, m):
            return l * N_SPLIT + m + 3

        @block.sync
        def _(sp):
            def load(l, n, b):
                sp.dma_start(raw[:, b, :], stream[bass.ds(l * N_STREAM + n, 1)].rearrange("o p f -> p (o f)")
                             ).then_inc(raw_loaded[b], 16)

            def load_split(l, n, b):
                sp.wait_ge(lo_ready, l * N_SPLIT + n - RAW - N_ADA + 1)
                load(l, n, b)

            sp.dma_start(const[:], const_in).then_inc(consts_loaded, 16)
            sp.dma_start(silu_c[:], c_in).then_inc(consts_loaded, 16)
            sp.dma_start(rel[:], rel_in).then_inc(consts_loaded, 16)
            sp.dma_start(onehot[:], onehot_in).then_inc(consts_loaded, 16)
            sp.dma_start(mask_s[:], mask_in).then_inc(consts_loaded, 16)
            for half in range(2):
                sp.sem_inc(gate_stored[half], 16)
            for l in range(DEPTH):
                if l:
                    sp.wait_ge(small_free, l)
                sp.dma_start(cols[:], cols_in[l]).then_inc(params_loaded, 16)
                sp.dma_start(rows[:], rows_in[l]).then_inc(params_loaded, 16)
                sp.dma_start(w2[:], w2_in[l]).then_inc(params_loaded, 16)
                for b in range(RAW):
                    if l:
                        sp.wait_ge(lo_ready, l * N_SPLIT - RAW + b + 1)
                    load(l, b, b)
                if l == 0:
                    sp.dma_start(x[:], x_in).then_inc(x_loaded, 16)
                with sp.Fori(1, N_ADA // RAW) as i:
                    for b in range(RAW):
                        sp.wait_ge(ada_used, l * N_ADA + (i - 1) * RAW + b + 1)
                        load(l, i * RAW + b, b)
                for b in range(RAW):
                    sp.wait_ge(ada_used, (l + 1) * N_ADA - RAW + b + 1)
                    load(l, N_ADA + b, b)
                if l == 0:
                    for h in range(SH):
                        sp.wait_ge(band_out, h + 1)
                        sp.dma_start(band_d[h].rearrange("(p c) -> p c", p=P), band[:, h, :]).then_inc(band_stored, 16)
                n0 = N_ADA // RAW
                with sp.Fori(n0 + 1, n0 + U_MIX // RAW + 1) as i:
                    for b in range(RAW):
                        load_split(l, i * RAW + b, b)
                sp.wait_ge(band_stored, 16 * SH)
                sp.wait_ge(bias_free, l + 1)
                for h in range(SH):
                    sp.dma_start(bias_s[:, h, :], band_d[h, P - 1:P - 1 + P * 383].rearrange(
                        "(q s) -> q s", s=383)[:, 0:256]).then_inc(bias_loaded, 16)
                with sp.Fori(n0 + U_MIX // RAW + 1, n0 + U_WQ // RAW) as i:
                    for b in range(RAW):
                        load_split(l, i * RAW + b, b)
                sp.wait_ge(h_ready, (2 * l + 2) * KC)
                sp.dma_start(sub_raw[:], sub_in[l]).then_inc(sub_loaded, 16)
                with sp.Fori(n0 + U_WQ // RAW, n0 + U_VE // RAW) as i:
                    for b in range(RAW):
                        load_split(l, i * RAW + b, b)
                def load_pair(pair, b):
                    src = bass.ds(pair * 2, 2)
                    sp.dma_start(a_in[:, b], act_d[src].rearrange("i j t -> j i t")).then_inc(ag_loaded[b], 16)
                    sp.dma_start(g_in[:, b].rearrange("p c i t -> p c (i t)"),
                                 gate_d[:, :, src].rearrange("c j i t -> j c (i t)")).then_inc(ag_loaded[b], 16)

                v0 = N_ADA + U_VE
                for b in range(RAW):
                    load_split(l, v0 + b, b)
                for half in range(2):
                    sp.wait_ge(gate_stored[half], 16 + (l + 1) * TT * 16)
                for s in range(2):
                    sp.wait_ge(gel_stored[s], 16 + (l + 1) * (NK // 2) * 16)
                sp.wait_ge(y_zero, l + 1)
                for b in range(4):
                    load_pair(b, b)
                for b in range(4):
                    sp.wait_ge(w_ready, l * (NK // 2) + b + 1)
                    load_pair(4 + b, b)
                for b in range(RAW):
                    load_split(l, v0 + RAW + b, b)
                with sp.Fori(1, NK // 8 - 1) as g:
                    for k in range(2):
                        for b in range(RAW):
                            load_split(l, g * 8 + (v0 + k * RAW + b), b)
                        for b in (2 * k, 2 * k + 1):
                            sp.wait_ge(w_ready, g * 4 + (l * (NK // 2) + b + 1))
                            load_pair(g * 4 + (4 + b), b)
                for k in range(2):
                    for b in range(RAW):
                        load_split(l, N_ADA + N_SPLIT - 8 + k * RAW + b, b)
            for tt in range(TT):
                sp.wait_ge(out_ready, tt + 1)
                sp.dma_start(out[tt * P:(tt + 1) * P, :], x[:, tt, :]).then_inc(out_stored, 16)
            sp.wait_ge(out_stored, 16 * TT)

        @block.scalar
        def _(act):
            step = Chain(act, act_step)

            def copy(o, i):
                return act.activation(o, i, ACT.Copy)

            def split_at(l, m, r, s, b):
                act.wait_ge(raw_loaded[b], (l * ROUNDS + r + 1) * 16)
                act.wait_ge(unit_used, used(l, m) - 2)
                copy(w_hi[:, s, :], raw[:, b, :]).then_inc(hi_ready, 1)

            def split_next(l, m):
                if m < N_SPLIT:
                    split_at(l, m, (N_ADA + m) // RAW, m % 2, m % RAW)

            def norm(k):
                if k == 0:
                    act.wait_ge(x_loaded, 16)
                    act.wait_ge(band_out, SH)
                else:
                    act.wait_ge(x_ready, k)
                for tt in range(TT):
                    act.activation(junk[:], x[:, tt, :], ACT.Square, accum_out=small[:, tt:tt + 1]
                                   ).then_inc(sumsq, 1)
                    act.wait_ge(sumsq, k * TT + tt + 1)
                act.wait_ge(meansq, k + 1)
                act.activation(small[:, 4:8], small[:, 4:8], ACT.Sqrt).then_inc(rstd, 1)
                for c in range(KC):
                    act.wait_ge(hf_ready, k * KC + c + 1)
                    copy(h_hi[:, c, :], hf[:, c % 2, :]).then_inc(hhi_ready, 1)

            def transposed_hi(dst, count):
                for c in range(KC):
                    act.wait_ge(tr_mm, count + c + 1)
                    copy(dst[:, c, :], ps[:, 4 + c % 4, :]).then_inc(tr_hi, 1)

            act.sem_inc(gel_stored[0], 16)
            act.sem_inc(gel_stored[1], 16)
            act.sem_inc(gate_ready, 2)
            act.wait_ge(consts_loaded, 80)
            act.activation(silu_c[:], silu_c[:], ACT.Silu).then_inc(silu_ready, 1)

            for l in range(DEPTH):
                norm(2 * l)
                split_next(l, 0)
                if l == 0:
                    act.wait_ge(band_stored, 16 * SH)
                for m in range(U_MIX):
                    split_next(l, m + 1)
                    act.wait_ge(unit_used, used(l, m))
                    bank = ps[:, ORDER[m] % 2, :] if m in ORDER else None
                    if m in range(U_Q, U_K):
                        copy(q_g[:, m - U_Q, :], bank).then_inc(col_act, 1)
                    elif m in range(U_K, U_LR):
                        copy(k_g[:, m - U_K, :], bank).then_inc(col_act, 1)
                    elif m == U_LR:
                        copy(lrT[:], bank[0:16]).then_inc(col_act, 1)
                    elif m in range(U_SQ, U_SK):
                        copy(qT_s[:, m - U_SQ, :], bank).then_inc(col_act, 1)
                    elif m in range(U_SK, U_SV):
                        copy(kT_s[:, m - U_SK, :], bank).then_inc(col_act, 1)
                    elif m == U_SV:
                        copy(vT_s[:], bank).then_inc(col_act, 1)
                    elif m in (U_V + 3, U_V + 7):
                        dh = (m - U_V) // 4
                        copy(v_g[:, :, dh * 512:dh * 512 + 512], ps[:, 4:8, :]).then_inc(row_done, 1)
                    elif m in (U_R + 3, U_R + 7):
                        dh = (m - U_R) // 4
                        act.activation(r_g[:, :, dh * 512:dh * 512 + 512], ps[:, 4:8, :], ACT.Silu
                                       ).then_inc(row_done, 1)
                for h in range(GH):
                    k = l * GH + h
                    gb = cols[:, V_GB + h:V_GB + h + 1]
                    act.wait_ge(gate_mm, k + 1)
                    if h:
                        act.wait_ge(keys_ready, k)
                    step(act.activation(tmp[:, 0, :], ps[:, 2 + h % 2, :], ACT.Abs, bias=gb))
                    step(act.activation(tmp[:, 0, :], tmp[:, 0, :], ACT.Exp, scale=-1.0))
                    act.activation(tmp[:, 0, :], tmp[:, 0, :], ACT.Ln, bias=1.0).then_inc(soft, 1)
                    act.wait_ge(decay, k + 1)
                    act.activation(tmp[:, 2, :], tmp[:, 1, :], ACT.Exp, scale=1.0 / GLA_TAU)
                    act.activation(tmp[:, 3, :], tmp[:, 1, :], ACT.Exp, scale=-1.0 / GLA_TAU)
                    for c in range(8):
                        act.activation(tmp[:, 4, c * 64:c * 64 + 64], tmp[:, 1, c * 64:c * 64 + 64], ACT.Exp,
                                       scale=-1.0 / GLA_TAU, bias=small[:, 8 + h * 8 + c:9 + h * 8 + c])
                    act.activation(small[:, 40 + h * 8:48 + h * 8], small[:, 8 + h * 8:16 + h * 8], ACT.Exp
                                   ).then_inc(decay_exp, 1)
                    act.wait_ge(tail_mm, k + 1)
                    copy(ktail[:, h], ps[:, 0, :].rearrange("p (a b) -> p a b", a=TT)).then_inc(tail_ready, 1)
                for p in range(TT):
                    k = l * TT + p
                    act.wait_ge(o_mm, k + 1)
                    for h in range(GH):
                        act.activation(tmp[:, h, 0:256], ps[:, 2 + h // 2, h % 2 * 256:h % 2 * 256 + 256],
                                       ACT.Square, accum_out=small[:, 72 + h:73 + h]).then_inc(o_sq, 1)
                    act.wait_ge(o_ms, k + 1)
                    act.activation(small[:, 76:80], small[:, 76:80], ACT.Sqrt).then_inc(o_rstd, 1)
                transposed_hi(oa_hi, l * 2 * KC)
                def square(t):
                    src = qT_s[:, t, :] if t < 8 else kT_s[:, t - 8, :]
                    if t >= 2:
                        act.wait_ge(sq_mm, l * 10 + t - 1)
                    act.activation(tmp[:, t % 2, :], src, ACT.Square).then_inc(sq_ready, 1)

                square(0)
                for t in range(10):
                    if t < 9:
                        square(t + 1)
                    act.wait_ge(sq_inv, l * 10 + t + 1)
                    act.activation(tmp[:, 2 + t % 2, :], tmp[:, 2 + t % 2, :], ACT.Sqrt).then_inc(sq_root, 1)

                def keep_pT(h):
                    k = l * SH + h
                    act.wait_ge(pT_mm, k + 1)
                    if h >= 2:
                        act.wait_ge(os_mm, k - 1)
                    copy(pT[:, h % 2], ps[:, 4:6, :].rearrange("p a (b c) -> p (a b) c", b=4)).then_inc(pT_ready, 1)

                for h in range(SH):
                    s = h % 2
                    act.wait_ge(logit_ready, l * SH + h + 1)
                    for b in range(TT):
                        act.activation(logit[:, s, b, :], logit[:, s, b, :], ACT.Exp,
                                       bias=small[:, 80 + 8 * s + b:81 + 8 * s + b],
                                       accum_out=small[:, 84 + 8 * s + b:85 + 8 * s + b])
                    act.activation(small[:, 96 + 4 * s:100 + 4 * s], small[:, 80 + 8 * s:84 + 8 * s], ACT.Exp,
                                   bias=rows[:, DV + h:DV + h + 1]).then_inc(prob_ready, 1)
                    if h:
                        keep_pT(h - 1)
                keep_pT(SH - 1)
                transposed_hi(ob_hi, l * 2 * KC + KC)
                for m in range(U_MIX, U_OUT):
                    split_next(l, m + 1)
                    if (m - U_MIX) % 2 == 0:
                        n = (m - U_MIX) // 2
                        act.wait_ge(unit_used, used(l, m))
                        if n >= 4:
                            act.wait_ge(col_dve, l * DVE_DONE + n - 3)
                        act.activation(sig[:, n % 4, :], ps[:, ORDER[m] % 2, :], ACT.Sigmoid).then_inc(col_act, 1)
                act.wait_ge(unit_used, used(l, U_OUT - 1))
                for c in range(KC):
                    act.wait_ge(mixed_sum, l * KC + c + 1)
                    copy(h_hi[:, c, :], mixedT[:, c, :]).then_inc(mixed_hi, 1)
                for m in range(U_OUT, U_WQ):
                    if m < U_WQ - 1:
                        split_next(l, m + 1)
                norm(2 * l + 1)
                split_next(l, U_WQ)
                act.wait_ge(sub_loaded, 16 * (l + 1))
                copy(sub_hi[:], sub_raw[:]).then_inc(subhi_ready, 1)

                def keep_scores(n):
                    act.wait_ge(score_mm, l * 16 + n + 1)
                    copy(scores[:, :, n, :], ps[:, 2 + n % 2, :].rearrange("p (a b) -> p a b", a=TT)
                         ).then_inc(score_ready, 1)

                for m in range(U_WQ, U_U):
                    n = m - U_WQ
                    split_next(l, m + 1)
                    act.wait_ge(unit_used, used(l, m))
                    if n >= 2:
                        act.wait_ge(score_mm, l * 16 + n - 1)
                    copy(q_hi[:, n % 2, :], ps[:, ORDER[m] % 2, :]).then_inc(qhi_ready, 1)
                    if n:
                        keep_scores(n - 1)
                keep_scores(15)

                def experts(i, n, first, extra=None):
                    for b in range(4):
                        mm = i * n + (U_U + first + b)
                        split_at(l, mm + 1, i * (n // RAW) + (N_ADA + U_U + first + b + 1) // RAW,
                                 (b + 1) % 2, (b + 1) % RAW)
                        act.wait_ge(unit_used, used(l, mm))
                        act.wait_ge(gel_stored[b % 2], i * (n * 8) + 16 * (l * NK + first + b - b % 2) // 2 + 16)
                        act.activation(gel[:, b % 2, :], ps[:, b % 2, :], ACT.Gelu_apprx_tanh).then_inc(col_act, 1)
                        if extra:
                            extra(b)
                        act.wait_ge(col_act, i * n + (l * ACT_DONE + DONE[U_U][1] + first + b))
                        act.dma_start(act_d[bass.ds(i * n + (first + b), 1)].rearrange("o j t -> j (o t)"),
                                      gel[:, b % 2, :]).then_inc(gel_stored[b % 2], 16)

                with act.Fori(0, 12) as i:
                    experts(i, 4, 0)
                for tt in range(TT):
                    def gate_exp(b):
                        if b == 1:
                            act.wait_ge(gexp_in, l * TT + tt + 1)
                            act.activation(best[:, tt], best[:, tt], ACT.Exp).then_inc(gexp, 1)

                    experts(0, 4, 48 + 4 * tt, gate_exp)
                    act.wait_ge(pick_mm, l * TT + tt + 1)
                    copy(idxT[:, tt, 0:2, :], ps[:, 4, 0:256].rearrange("p (a b) -> p a b", a=2))
                    copy(g_round[:, tt, :], ps[:, 4, 256:384]).then_inc(ghi_ready, 1)
                with act.Fori(0, TT) as tt:
                    def gates(k):
                        def extra(b):
                            for g in range(2):
                                n = (k * 4 + b) * 2 + g
                                half = n // 16
                                act.wait_ge(hot_used, tt * 32 + (l * P + n + 1 + 2))
                                if n % 16 == 0:
                                    act.wait_ge(gate_stored[half], tt * 16 + (l * TT * 16 + 16))
                                t = 4 * (n % 16)
                                copy(gatebuf[:, half, :, t:t + 4],
                                     ps[:, 4 + n % 2, :].rearrange("p (t i) -> p i t", t=4)).then_inc(gate_ready, 1)
                                if n % 16 == 15:
                                    act.wait_ge(gate_ready, tt * 32 + (l * P + n + 1 + 2))
                                    act.dma_start(gate_d[bass.ds(tt * 2 + half, 1)].rearrange("o j i t -> j (o i t)"),
                                                  gatebuf[:, half].rearrange("p i t -> p (i t)")
                                                  ).then_inc(gate_stored[half], 16)
                        return extra
                    for k in range(4):
                        experts(tt, 16, 64 + 4 * k, gates(k))
                def pair_hi(g, kk, s):
                    act.wait_ge(w_prod, g * 4 + (l * 64 + kk + 1))
                    act.wait_ge(unit_used, used(l, U_VE - 1) + (g * 8 - 8 if not isinstance(g, int) else max(g * 8 - 8, 0)))
                    copy(g_hi[:, s, 2 * kk:2 * kk + 2, :], a_in[:, kk]).then_inc(w_hi_ready, 1)

                def sum_group(g, s, last=False):
                    for u in range(8):
                        if not (last and u == 7):
                            split_at(l, g * 8 + (U_VE + u + 1), g * 2 + (N_ADA + U_VE + u + 1) // RAW, (u + 1) % 2,
                                     (u + 1) % RAW)
                        if u % 2 and not last:
                            pair_hi(g + 1, u // 2, 1 - s)

                for kk in range(4):
                    pair_hi(0, kk, 0)
                with act.Fori(0, 7) as i:
                    sum_group(i * 2, 0)
                    sum_group(i * 2 + 1, 1)
                sum_group(14, 0)
                sum_group(15, 1, last=True)

        @block.gpsimd
        def _(pool):
            def split(m, b):
                pool.wait_ge(hi_ready, m + 1)
                pool.tensor_tensor(w_lo[:, b % 2, :], raw[:, b, :], w_hi[:, b % 2, :].bitcast(F32), ALU.subtract
                                   ).then_inc(lo_ready, 1)

            def product(l, g, b):
                pool.wait_ge(ag_loaded[b], g * 32 + (l * 512 + 32))
                a4 = a_in[:, b].rearrange("p i (c t) -> p c i t", t=GT)
                pool.tensor_tensor(a4, a4, g_in[:, b], ALU.mult).then_inc(w_prod, 1)

            for l in range(DEPTH):
                with pool.Fori(0, U_VE // RAW) as i:
                    for b in range(RAW):
                        split(i * RAW + (l * N_SPLIT + b), b)
                for b in range(RAW):
                    product(l, 0, b)
                v0 = l * N_SPLIT + U_VE
                with pool.Fori(0, 15) as g:
                    for u in range(8):
                        split(g * 8 + (v0 + u), u % RAW)
                        if u % 2:
                            product(l, g + 1, u // 2)
                for u in range(8):
                    split(v0 + 120 + u, u % RAW)

        @block.tensor
        def _(pe):
            def column_unit(m, bank, s, mov_hi, mov_lo, width=P):
                o = ps[0:width, bank, :]
                for c in range(KC):
                    w = slice(c * P, c * P + width)
                    pe.matmul(o, w_hi[:, s, w], mov_hi[:, c, :], start=c == 0, stop=False)
                    pe.matmul(o, w_lo[:, s, w], mov_hi[:, c, :], start=False, stop=False)
                    mm = pe.matmul(o, w_hi[:, s, w], mov_lo[:, c, :], start=False, stop=c == KC - 1)
                mm.then_inc(unit_used, 1)

            def row_unit(q, bank0, s, sta_hi, sta_lo):
                for kk in range(2):
                    w = slice(kk * 512, kk * 512 + 512)
                    for tt in range(TT):
                        t = slice(tt * P, tt * P + P)
                        first, last = q == 0 and kk == 0, q == 3 and kk == 1
                        o = ps[:, bank0 + tt, :]
                        pe.matmul(o, sta_hi[:, 2 * q + kk, t], w_hi[:, s, w], start=first, stop=False)
                        pe.matmul(o, sta_hi[:, 2 * q + kk, t], w_lo[:, s, w], start=False, stop=False)
                        mm = pe.matmul(o, sta_lo[:, 2 * q + kk, t], w_hi[:, s, w], start=False, stop=last)
                mm.then_inc(unit_used, 1)

            def column(l, m, mov_hi, mov_lo, width=P):
                pe.wait_ge(lo_ready, l * N_SPLIT + m + 1)
                n = ORDER[m]
                if n >= 2:
                    eng, count = DONE[COLUMN_UNITS[n - 2][0]]
                    if eng == "act":
                        pe.wait_ge(col_act, l * ACT_DONE + count)
                    else:
                        pe.wait_ge(col_dve, l * DVE_DONE + count)
                column_unit(m, n % 2, m % 2, mov_hi, mov_lo, width)

            def norm(k):
                for c in range(KC):
                    if c == 0:
                        pe.wait_ge(xn_ready, (k + 1) * TT)
                    if c >= 4:
                        pe.wait_ge(hf_ready, k * KC + c - 3)
                    for tt in range(TT):
                        mm = pe.transpose(ps[:, 4 + c % 4, tt * P:(tt + 1) * P], xn[:, tt, c * P:(c + 1) * P], ident)
                    mm.then_inc(xT_mm, 1)

            def transposed(src, count):
                for c in range(KC):
                    if c >= 4:
                        pe.wait_ge(tr_done, count + c - 3)
                    for tt in range(TT):
                        mm = pe.transpose(ps[:, 4 + c % 4, tt * P:(tt + 1) * P], src[:, tt, c * P:(c + 1) * P], ident)
                    mm.then_inc(tr_mm, 1)

            pe.sem_inc(unit_used, 2)
            pe.sem_inc(hot_used, 2)
            pe.wait_ge(rel_rep, 1)
            for h in range(SH):
                if h >= 2:
                    pe.wait_ge(band_out, h - 1)
                pe.matmul(ps[:, h % 2, 0:384], rel_b[:, h, :], onehot[:], start=True, stop=True).then_inc(band_mm, 1)
            pe.wait_ge(silu_ready, 1)
            for l in range(DEPTH):
                if l:
                    pe.wait_ge(x_ready, 2 * l)
                with pe.Fori(0, N_ADA // RAW) as i:
                    for b in range(RAW):
                        pe.wait_ge(raw_loaded[b], i * 16 + (l * ROUNDS * 16 + 16))
                        for c in range(KC):
                            mm = pe.matmul(ps[:, 2, bass.ds(i * RAW + b, 1)], raw[:, b, c * P:(c + 1) * P],
                                           silu_c[:, c:c + 1], start=c == 0, stop=c == KC - 1)
                        mm.then_inc(ada_used, 1)
                pe.wait_ge(diag_ready, l + 1)
                for j in range(16):
                    mm = pe.matmul(ps[:, 4 + j // 4, j % 4 * P:j % 4 * P + P], const[:, C_ONES:C_ONES + P], diag[:, j, :],
                                   start=True, stop=True)
                mm.then_inc(grow_mm, 1)
                norm(2 * l)
                pe.wait_ge(h_ready, (2 * l + 1) * KC)
                for m in range(U_MIX):
                    if m in ORDER:
                        column(l, m, h_hi, h_lo, 16 if m == U_LR else P)
                    else:
                        j = (m - U_V) // 4 if m < U_SQ else 2 + (m - U_R) // 4
                        q = (m - U_V) % 4 if m < U_SQ else (m - U_R) % 4
                        pe.wait_ge(lo_ready, l * N_SPLIT + m + 1)
                        if q == 0 and j:
                            pe.wait_ge(row_done, l * 4 + j)
                        row_unit(q, 4, m % 2, h_hi, h_lo)
                pe.wait_ge(params_loaded, (l + 1) * 48)
                pe.wait_ge(col_act, l * ACT_DONE + DONE[U_SV][1])

                def gate(h):
                    if h >= 2:
                        pe.wait_ge(decay, l * GH + h - 1)
                    pe.matmul(ps[:, 2 + h % 2, :], w2[:, h * P:(h + 1) * P], lrT[:], start=True, stop=True
                              ).then_inc(gate_mm, 1)

                gate(0)
                for h in range(GH):
                    k = l * GH + h
                    if h < GH - 1:
                        gate(h + 1)
                    pe.wait_ge(keys_ready, k + 1)
                    if h:
                        pe.wait_ge(tail_ready, k)
                    for p in range(TT):
                        mm = pe.transpose(ps[:, 0, p * P:(p + 1) * P], k_g[:, h, p * P:(p + 1) * P], ident)
                    mm.then_inc(tail_mm, 1)
                pe.wait_ge(row_done, l * 4 + 4)
                for p in range(TT):
                    k = l * TT + p
                    if p:
                        pe.wait_ge(attn_ready, k)
                    for h in range(GH):
                        mm = pe.matmul(ps[:, 1, h * P:(h + 1) * P], kinv[:, h, p * P:(p + 1) * P],
                                       q_g[:, h, p * P:(p + 1) * P], start=True, stop=True)
                    mm.then_inc(attn_mm, 1)
                    if p == 0:
                        pe.wait_ge(tail_ready, l * GH + GH)
                    for e in range(2):
                        c = 2 * p + e
                        if c == 7:
                            break
                        if c >= 2:
                            pe.wait_ge(state_ready, l * 7 + c - 1)
                        r = slice(64 * e, 64 * e + 64)
                        for h in range(GH):
                            mm = pe.matmul(ps[:, 4 + 2 * e + h // 2, h % 2 * 256:h % 2 * 256 + 256], ktail[r, h, p, :],
                                           v_g[r, p, h * DV:(h + 1) * DV], start=True, stop=True)
                        mm.then_inc(upd_mm, 1)
                    pe.wait_ge(attn_ready, k + 1)
                    pe.wait_ge(state_ready, l * 7 + 2 * p + 1)
                    if p:
                        pe.wait_ge(o_done, k)
                    for h in range(GH):
                        o = ps[:, 2 + h // 2, h % 2 * 256:h % 2 * 256 + 256]
                        t0 = p * P
                        pe.matmul(o, attnT[:, p % 2, h, :], v_g[:, p, h * DV:(h + 1) * DV], start=True, stop=False,
                                  skip_group_check=True)
                        if p:
                            pe.matmul(o[0:64], q_g[:, h, t0:t0 + 64], state[:, 0, h, :], start=False, stop=False,
                                      skip_group_check=True)
                        mm = pe.matmul(o[64:128], q_g[:, h, t0 + 64:t0 + 128], state[:, 1, h, :], start=False, stop=True,
                                       skip_group_check=True)
                    mm.then_inc(o_mm, 1)
                pe.wait_ge(o_done, (l + 1) * TT)
                transposed(r_g, l * 2 * KC)
                for t in range(10):
                    pe.wait_ge(sq_ready, l * 10 + t + 1)
                    if t >= 2:
                        pe.wait_ge(sq_inv, l * 10 + t - 1)
                    pe.matmul(ps[:, t % 2, :], const[:, C_HEADS:C_HEADS + P], tmp[:, t % 2, :], start=True, stop=True
                              ).then_inc(sq_mm, 1)
                pe.wait_ge(tr_done, l * 2 * KC + KC)
                for b in range(TT):
                    mm = pe.transpose(ps[:, 6, b * P:(b + 1) * P], vT_s[:, b * P:(b + 1) * P], ident)
                mm.then_inc(vs_mm, 1)
                pe.wait_ge(sqk_ready, (l + 1) * 10)

                def logits(h):
                    if h >= 2:
                        pe.wait_ge(logit_ready, l * SH + h - 1)
                    r = slice(HD * (h % 2), HD * (h % 2) + HD)
                    kv = h // 8
                    for b in range(TT):
                        o = ps[:, 2 * (h % 2) + b // 2, b % 2 * 256:b % 2 * 256 + 256]
                        q = qT_s[r, h // 2, b * P:(b + 1) * P]
                        if b == 0:
                            mm = pe.matmul(o[:, 128:256], q, kT_s[r, kv, 0:P], start=True, stop=True)
                        else:
                            mm = pe.matmul(o, q, kT_s[r, kv, (b - 1) * P:(b + 1) * P], start=True, stop=True)
                    mm.then_inc(logit_mm, 1)

                def probs(h):
                    pe.wait_ge(prob_ready, l * SH + h + 1)
                    if h:
                        pe.wait_ge(pT_ready, l * SH + h)
                    for j in range(1, 8):
                        mm = pe.transpose(ps[:, 4 + j // 4, j % 4 * P:j % 4 * P + P],
                                          logit[:, h % 2, j // 2, j % 2 * P:j % 2 * P + P], ident)
                    mm.then_inc(pT_mm, 1)

                def values(h):
                    pe.wait_ge(pT_ready, l * SH + h + 1)
                    if h == 0:
                        pe.wait_ge(vs_ready, l + 1)
                    if h >= 2:
                        pe.wait_ge(os_ready, l * SH + h - 1)
                    kv = slice(h // 8 * HD, h // 8 * HD + HD)
                    for b in range(TT):
                        o = ps[:, 6 + h % 2, b * HD:b * HD + HD]
                        if b:
                            pe.matmul(o, pT[:, h % 2, 2 * b, :], v_s[:, b - 1, kv], start=True, stop=False)
                        mm = pe.matmul(o, pT[:, h % 2, 2 * b + 1, :], v_s[:, b, kv], start=b == 0, stop=True)
                    mm.then_inc(os_mm, 1)

                logits(0)
                for h in range(SH):
                    if h < SH - 1:
                        logits(h + 1)
                    probs(h)
                    if h:
                        values(h - 1)
                values(SH - 1)
                pe.wait_ge(os_ready, (l + 1) * SH)
                transposed(o_s, l * 2 * KC + KC)
                pe.wait_ge(tr_done, (l + 1) * 2 * KC)
                for m in range(U_MIX, U_OUT):
                    kind = (m - U_MIX) % 4
                    mov = {0: (h_hi, h_lo), 1: (oa_hi, oa_lo), 2: (h_hi, h_lo), 3: (ob_hi, ob_lo)}[kind]
                    column(l, m, *mov)
                for m in range(U_OUT, U_WQ):
                    q, j = (m - U_OUT) % 4, (m - U_OUT) // 4
                    pe.wait_ge(lo_ready, l * N_SPLIT + m + 1)
                    if j == 0:
                        pe.wait_ge(mixed_ready, l * KC + 2 * q + 2)
                    elif q == 0:
                        pe.wait_ge(row_dve, l * 2 + 1)
                    row_unit(q, 4, m % 2, h_hi, h_lo)
                norm(2 * l + 1)
                pe.wait_ge(h_ready, (2 * l + 2) * KC)

                def score(n):
                    pe.wait_ge(col_dve, l * DVE_DONE + 16 + n + 1)
                    if n == 0:
                        pe.wait_ge(sub_ready, l + 1)
                    if n >= 2:
                        pe.wait_ge(score_ready, l * 16 + n - 1)
                    k = slice(n % 2 * P, n % 2 * P + P)
                    for tt in range(TT):
                        t = slice(tt * P, tt * P + P)
                        o = ps[:, 2 + n % 2, t]
                        pe.matmul(o, q_hi[:, n % 2, t], sub_hi[:, k], start=True, stop=False)
                        pe.matmul(o, q_hi[:, n % 2, t], sub_lo[:, k], start=False, stop=False)
                        mm = pe.matmul(o, q_lo[:, n % 2, t], sub_hi[:, k], start=False, stop=True)
                    mm.then_inc(score_mm, 1)

                for n in range(16):
                    column(l, U_WQ + n, h_hi, h_lo)
                    if n:
                        score(n - 1)
                score(15)

                def experts(i, n, first, extra=None):
                    for b in range(4):
                        e = i * n + (first + b)
                        pe.wait_ge(lo_ready, e + (l * N_SPLIT + U_U + 1))
                        pe.wait_ge(col_act, e + (l * ACT_DONE + DONE[U_U][1] - 2))
                        column_unit(None, b % 2, b % 2, h_hi, h_lo)
                        if extra:
                            extra(b)

                with pe.Fori(0, 12) as i:
                    experts(i, 4, 0)
                for tt in range(TT):
                    experts(0, 4, 48 + 4 * tt)
                    pe.wait_ge(picked_ready, l * TT + tt + 1)
                    if tt:
                        pe.wait_ge(idx_ready, l * TT + tt)
                    for r in range(3):
                        mm = pe.transpose(ps[:, 4, r * P:(r + 1) * P], picked[:, r, :], ident)
                    mm.then_inc(pick_mm, 1)
                pe.wait_ge(idx_ready, (l + 1) * TT)
                with pe.Fori(0, TT) as tt:
                    def gates(k):
                        def extra(b):
                            for g in range(2):
                                n = (k * 4 + b) * 2 + g
                                pe.wait_ge(hot_ready, tt * 32 + (l * P + n + 1))
                                pe.wait_ge(gate_ready, tt * 32 + (l * P + n + 1))
                                for q in range(4):
                                    o = ps[:, 4 + n % 2, q * P:(q + 1) * P]
                                    pe.matmul(o, hot_j[:, n % 2, q, :], hot_i[:, n % 2, q, 0, :], start=True, stop=False)
                                    mm = pe.matmul(o, hot_j[:, n % 2, q, :], hot_i[:, n % 2, q, 1, :], start=False,
                                                   stop=True)
                                mm.then_inc(hot_used, 1)
                        return extra
                    for k in range(4):
                        experts(tt, 16, 64 + 4 * k, gates(k))

                def sum_group(g, s):
                    pe.wait_ge(w_ready, g * 4 + (l * 64 + 4))
                    for u in range(8):
                        pe.wait_ge(lo_ready, g * 8 + (l * N_SPLIT + U_VE + u + 1))
                        if u % 4 == 0:
                            pe.wait_ge(y_done, g * 2 + (l * 32 + u // 4 + 1))
                        row_unit(u % 4, u // 4 * 4, u % 2, g_hi[:, s], g_lo[:, s])

                with pe.Fori(0, 8) as i:
                    sum_group(i * 2, 0)
                    sum_group(i * 2 + 1, 1)

        @block.vector
        def _(dve):
            step = Chain(dve, dve_step)
            tt_op = dve.tensor_tensor

            def settle(ins):
                step(ins)
                dve.sem_inc(fence, 1)

            def norm(k, scale0, shift0):
                dve.wait_ge(sumsq, (k + 1) * TT)
                step(dve.tensor_scalar(small[:, 4:8], small[:, 0:4], 1.0 / D, EPS, ALU.mult, ALU.add))
                dve.reciprocal(small[:, 4:8], small[:, 4:8]).then_inc(meansq, 1)
                dve.wait_ge(rstd, k + 1)
                for tt in range(TT):
                    dve.tensor_scalar(xn[:, tt, :], x[:, tt, :], small[:, 4 + tt:5 + tt], None, ALU.mult
                                      ).then_inc(xn_ready, 1)
                for c in range(KC):
                    dve.wait_ge(xT_mm, k * KC + c + 1)
                    if c >= 2:
                        dve.wait_ge(h_ready, k * KC + c - 1)
                    dve.tensor_scalar(hf[:, c % 2, :], ps[:, 4 + c % 4, :], mod[:, scale0 + c:scale0 + c + 1],
                                      mod[:, shift0 + c:shift0 + c + 1], ALU.mult, ALU.add).then_inc(hf_ready, 1)
                    if c:
                        norm_lo(k, c - 1)
                norm_lo(k, KC - 1)

            def norm_lo(k, c):
                dve.wait_ge(hhi_ready, k * KC + c + 1)
                tt_op(h_lo[:, c, :], hf[:, c % 2, :], h_hi[:, c, :].bitcast(F32), ALU.subtract).then_inc(h_ready, 1)

            def transposed_lo(dst, hi, count):
                for c in range(KC):
                    dve.wait_ge(tr_hi, count + c + 1)
                    tt_op(dst[:, c, :], ps[:, 4 + c % 4, :], hi[:, c, :].bitcast(F32), ALU.subtract).then_inc(tr_done, 1)

            dve.sem_inc(y_done, 2)
            dve.wait_ge(consts_loaded, 80)
            dve.tensor_copy(rel_b[:], rel[:].unsqueeze(2).to_broadcast([32, SH, P])).then_inc(rel_rep, 1)
            for h in range(SH):
                dve.wait_ge(band_mm, h + 1)
                tt_op(band[:, h, :], ps[:, h % 2, 0:384], mask_s[:], ALU.add).then_inc(band_out, 1)

            for l in range(DEPTH):
                dve.wait_ge(params_loaded, (l + 1) * 48)
                dve.wait_ge(ada_used, (l + 1) * N_ADA)
                step(tt_op(mod[:], ps[:, 2, 0:N_ADA], cols[:, V_BADA:V_BADA + N_ADA], ALU.add))
                for a, v in ((8, V_N1), (32, V_N2)):
                    dve.scalar_tensor_tensor(out=mod[:, a:a + 8], in0=mod[:, a:a + 8], scalar=1.0,
                                             in1=cols[:, v:v + 8], op0=ALU.add, op1=ALU.mult)
                dve.tensor_scalar(cols[:, V_QN:V_QN + 1], cols[:, V_QN:V_QN + 1], HD ** -0.5, None, ALU.mult)
                for j in range(16):
                    g = (16 if j < 8 else 40) + j % 8
                    ins = dve.tensor_scalar(diag[:, j, :], ident, mod[:, g:g + 1], None, ALU.mult)
                ins.then_inc(diag_ready, 1)
                dve.wait_ge(grow_mm, l + 1)
                step(dve.tensor_copy(grow[:], ps[:, 4:8, :].rearrange("p (a b) c -> p a (b c)", a=2)))
                norm(2 * l, 8, 0)
                dve.wait_ge(row_done, l * 4 + 4)
                r16 = r_g[:].rearrange("p t (h v) -> p (t h) v", h=GH)
                step(tt_op(r16, r16, rows[:, 0:DV].unsqueeze(1).to_broadcast([P, 16, DV]), ALU.mult))
                for h in range(GH):
                    k = l * GH + h
                    dve.wait_ge(soft, k + 1)
                    step(dve.tensor_scalar(tmp[:, 1, :], ps[:, 2 + h % 2, :], cols[:, V_GB + h:V_GB + h + 1], 0.0,
                                           ALU.add, ALU.min))
                    step(tt_op(tmp[:, 2, :], tmp[:, 1, :], tmp[:, 0, :], ALU.subtract))
                    step(dve.tensor_tensor_scan(tmp[:, 1, :], const[:, C_SCAN:C_SCAN + SEQ], tmp[:, 2, :], 0.0,
                                                ALU.mult, ALU.add))
                    dve.tensor_scalar(small[:, 8 + h * 8:16 + h * 8], tmp[:, 1, CHUNK - 1:SEQ:CHUNK], 1.0 / GLA_TAU, None,
                                      ALU.mult).then_inc(decay, 1)
                    dve.wait_ge(decay_exp, k + 1)
                    dve.scalar_tensor_tensor(out=q_g[:, h, :], in0=q_g[:, h, :], scalar=DK ** -0.5, in1=tmp[:, 2, :],
                                             op0=ALU.mult, op1=ALU.mult)
                    tt_op(kinv[:, h, :], k_g[:, h, :], tmp[:, 3, :], ALU.mult)
                    tt_op(k_g[:, h, :], k_g[:, h, :], tmp[:, 4, :], ALU.mult).then_inc(keys_ready, 1)
                    dve.wait_ge(keys_ready, k + 1)
                step(dve.memset(attnT[:], 0.0))
                mask = const[:, C_CAUSAL:C_CAUSAL + P].bitcast(U32).unsqueeze(1).to_broadcast([P, GH, P])

                def update(c):
                    dve.wait_ge(upd_mm, l * 7 + c + 1)
                    if c == 1:
                        dve.wait_ge(o_mm, l * TT + 1)
                    elif c > 1:
                        dve.wait_ge(o_mm, l * TT + (c + 1) // 2)
                    for h in range(GH):
                        u = ps[:, 4 + 2 * (c % 2) + h // 2, h % 2 * 256:h % 2 * 256 + 256]
                        new = state[:, (c + 1) % 2, h, :]
                        if c == 0:
                            ins = dve.tensor_copy(new, u)
                        else:
                            ins = dve.scalar_tensor_tensor(out=new, in0=state[:, c % 2, h, :],
                                                           scalar=small[:, 40 + h * 8 + c:41 + h * 8 + c], in1=u,
                                                           op0=ALU.mult, op1=ALU.add)
                    ins.then_inc(state_ready, 1)
                    dve.wait_ge(state_ready, l * 7 + c + 1)

                for p in range(TT):
                    k = l * TT + p
                    dve.wait_ge(attn_mm, k + 1)
                    if p >= 2:
                        dve.wait_ge(o_mm, k - 1)
                    dve.copy_predicated(attnT[:, p % 2], mask, ps[:, 1, :].rearrange("p (a b) -> p a b", a=GH)
                                        ).then_inc(attn_ready, 1)
                    update(2 * p)
                    dve.wait_ge(o_sq, l * 16 + 4 * (p + 1))
                    if p:
                        dve.wait_ge(o_done, k)
                    step(dve.tensor_scalar(small[:, 76:80], small[:, 72:76], 1.0 / DV, EPS, ALU.mult, ALU.add))
                    dve.reciprocal(small[:, 76:80], small[:, 76:80]).then_inc(o_ms, 1)
                    if p < TT - 1:
                        update(2 * p + 1)
                    dve.wait_ge(o_rstd, k + 1)
                    for h in range(GH):
                        r = r_g[:, p, h * DV:(h + 1) * DV]
                        ins = dve.scalar_tensor_tensor(out=r, in0=ps[:, 2 + h // 2, h % 2 * 256:h % 2 * 256 + 256],
                                                       scalar=small[:, 76 + h:77 + h], in1=r, op0=ALU.mult, op1=ALU.mult)
                    ins.then_inc(o_done, 1)
                transposed_lo(oa_lo, oa_hi, l * 2 * KC)
                for t in range(10):
                    src = qT_s[:, t, :] if t < 8 else kT_s[:, t - 8, :]
                    g = cols[:, V_QN:V_QN + 1] if t < 8 else cols[:, V_KN:V_KN + 1]
                    s = tmp[:, 2 + t % 2, :]
                    dve.wait_ge(sq_mm, l * 10 + t + 1)
                    if t >= 2:
                        dve.wait_ge(sqk_ready, l * 10 + t - 1)
                    step(dve.tensor_scalar(s, ps[:, t % 2, :], EPS, None, ALU.add))
                    dve.reciprocal(s, s).then_inc(sq_inv, 1)
                    dve.wait_ge(sq_root, l * 10 + t + 1)
                    dve.scalar_tensor_tensor(out=src, in0=src, scalar=g, in1=s, op0=ALU.mult, op1=ALU.mult
                                             ).then_inc(sqk_ready, 1)
                dve.wait_ge(vs_mm, l + 1)
                dve.tensor_copy(v_s[:], ps[:, 6, :].rearrange("p (a b) -> p a b", a=TT)).then_inc(vs_ready, 1)
                dve.wait_ge(sqk_ready, (l + 1) * 10)
                dve.sem_inc(bias_free, 1)
                dve.wait_ge(bias_loaded, (l + 1) * 16 * SH)

                def finish(h):
                    s = h % 2
                    den = small[:, 84 + 8 * s:88 + 8 * s]
                    dve.wait_ge(prob_ready, l * SH + h + 1)
                    step(tt_op(den, den, small[:, 96 + 4 * s:100 + 4 * s], ALU.add))
                    step(dve.reciprocal(den, den))
                    dve.wait_ge(os_mm, l * SH + h + 1)
                    tt_op(o_s[:, :, h * HD:(h + 1) * HD], ps[:, 6 + s, 0:256].rearrange("p (a b) -> p a b", a=TT),
                          den.unsqueeze(2).to_broadcast([P, TT, HD]), ALU.mult).then_inc(os_ready, 1)

                for h in range(SH):
                    k, s = l * SH + h, h % 2
                    lp = ps[:, 2 * s:2 * s + 2, :].rearrange("p a (b c) -> p (a b) c", b=2)
                    dve.wait_ge(logit_mm, k + 1)
                    if h >= 2:
                        dve.wait_ge(pT_mm, k - 1)
                    dve.memset(logit[:, s, 0, 0:P], NEG)
                    tt_op(logit[:, s, 0, P:2 * P], lp[:, 0, P:2 * P], bias_s[:, h, P:2 * P], ALU.add)
                    step(tt_op(logit[:, s, 1:4, :], lp[:, 1:4, :], bias_s[:, h, :].unsqueeze(1).to_broadcast([P, 3, 256]),
                               ALU.add))
                    mx = small[:, 80 + 8 * s:84 + 8 * s]
                    step(dve.tensor_reduce(mx, logit[:, s], AX_X, ALU.max))
                    dve.tensor_scalar(mx, mx, rows[:, DV + h:DV + h + 1], -1.0, ALU.max, ALU.mult).then_inc(logit_ready, 1)
                    if h:
                        finish(h - 1)
                finish(SH - 1)
                transposed_lo(ob_lo, ob_hi, l * 2 * KC + KC)
                for m in range(U_MIX, U_OUT):
                    kind, c = (m - U_MIX) % 4, (m - U_MIX) // 4
                    if kind % 2:
                        dve.wait_ge(unit_used, used(l, m))
                        dve.wait_ge(col_act, l * ACT_DONE + DONE[m - 1][1])
                        j = kind // 2
                        if j == 0 and c:
                            dve.wait_ge(mixed_sum, l * KC + c)
                        tt_op(part[:, j, :], ps[:, ORDER[m] % 2, :], sig[:, (m - U_MIX) // 2 % 4, :], ALU.mult
                              ).then_inc(col_dve, 1)
                        if j:
                            dve.wait_ge(col_dve, l * DVE_DONE + DONE[m][1])
                            tt_op(mixedT[:, c, :], part[:, 0, :], part[:, 1, :], ALU.add).then_inc(mixed_sum, 1)
                for c in range(KC):
                    dve.wait_ge(mixed_hi, l * KC + c + 1)
                    tt_op(h_lo[:, c, :], mixedT[:, c, :], h_hi[:, c, :].bitcast(F32), ALU.subtract).then_inc(mixed_ready, 1)
                for m in range(U_OUT, U_WQ):
                    if (m - U_OUT) % 4 == 3:
                        dh = (m - U_OUT) // 4
                        dve.wait_ge(unit_used, used(l, m))
                        w = slice(dh * 512, dh * 512 + 512)
                        tt_op(xadd[:], ps[:, 4:8, :], grow[:, 0, w].unsqueeze(1).to_broadcast([P, TT, 512]), ALU.mult
                              ).then_inc(row_dve, 1)
                        dve.wait_ge(row_dve, l * 2 + dh + 1)
                        ins = tt_op(x[:, :, w], x[:, :, w], xadd[:], ALU.add)
                        if dh == 0:
                            step(ins)
                ins.then_inc(x_ready, 1)
                dve.wait_ge(x_ready, 2 * l + 1)
                norm(2 * l + 1, 32, 24)
                dve.wait_ge(subhi_ready, l + 1)
                tt_op(sub_lo[:], sub_raw[:], sub_hi[:].bitcast(F32), ALU.subtract).then_inc(sub_ready, 1)
                for m in range(U_WQ, U_U):
                    n = m - U_WQ
                    dve.wait_ge(qhi_ready, l * 16 + n + 1)
                    tt_op(q_lo[:, n % 2, :], ps[:, ORDER[m] % 2, :], q_hi[:, n % 2, :].bitcast(F32), ALU.subtract
                          ).then_inc(col_dve, 1)

                def top16(vals, rest_v, tops, idx, count):
                    for j in range(count):
                        ins = dve.max(tops(j)[:, 0:8], vals(j))
                    settle(ins)
                    for j in range(count):
                        ins = dve.match_replace(rest_v(j), tops(j)[:, 0:8], vals(j), LOWEST)
                    settle(ins)
                    for j in range(count):
                        ins = dve.max(tops(j)[:, 8:16], rest_v(j))
                        dve.max_index(idx(j)[:, 0:8], tops(j)[:, 0:8], vals(j))
                    settle(ins)
                    for j in range(count):
                        ins = dve.max_index(idx(j)[:, 8:16], tops(j)[:, 8:16], rest_v(j))
                    settle(ins)

                dve.wait_ge(score_ready, (l + 1) * 16)
                with dve.Fori(0, PH) as i:
                    step.enter(i, 11)
                    settle(dve.tensor_copy(pair_s[:], scores[:, :, bass.ds(i * 2, 2), :]))
                    for side in range(2):
                        top16(lambda j: pair_s[:, j, side, :], lambda j: pair_r[:, j, side, :],
                              lambda j: pair_t[:, j, side, :], lambda j: pair_i[:, j, side, :], TT)
                    step(dve.tensor_copy(top[:, :, bass.ds(i * 2, 2), :], pair_t[:]))
                    step(dve.tensor_copy(topf[:, :, bass.ds(i * 2, 2), :], pair_i[:]))
                    step.leave(PH)
                with dve.Fori(0, PH) as i:
                    step.enter(i, 6)
                    s1 = top[:, :, bass.ds(i * 2, 1), :].rearrange("p t o a -> p t (o a)")
                    s2 = top[:, :, bass.ds(i * 2 + 1, 1), :].rearrange("p t o a -> p t (o a)")
                    for tt in range(TT):
                        ins = tt_op(cand[:, tt, :].rearrange("p (a b) -> p a b", a=TOPK),
                                    s1[:, tt, :].unsqueeze(2).to_broadcast([P, TOPK, TOPK]),
                                    s2[:, tt, :].unsqueeze(1).to_broadcast([P, TOPK, TOPK]), ALU.add)
                    settle(ins)
                    top16(lambda j: cand[:, j, :], lambda j: rest[:, j, :], lambda j: pair_t[:, j, 0, :],
                          lambda j: pair_i[:, j, 0, :], TT)
                    dve.tensor_copy(best[:, :, bass.ds(i, 1), :], pair_t[:, :, 0:1, :])
                    step(dve.tensor_copy(posi[:, :, bass.ds(i, 1), :], pair_i[:, :, 0:1, :]))
                    step.leave(PH)

                def pick_rows(tt):
                    dve.wait_ge(ghi_ready, l * TT + tt + 1)
                    dve.tensor_copy(idxT[:, tt, 2, :], g_round[:, tt, :].bitcast(F32))
                    tt_op(idxT[:, tt, 3, :], ps[:, 4, 256:384], g_round[:, tt, :].bitcast(F32), ALU.subtract
                          ).then_inc(idx_ready, 1)

                iota16 = const[:, C_IOTA:C_IOTA + TOPK].unsqueeze(1).to_broadcast([P, PICKS, TOPK])
                for tt in range(TT):
                    for b in range(4):
                        if b == 0:
                            step(dve.tensor_copy(gden[:, 8:16], best[:, tt, :, 0]))
                            tt_op(best[:, tt], best[:, tt], gden[:, 8:16].unsqueeze(2).to_broadcast([P, PH, TOPK]),
                                  ALU.subtract).then_inc(gexp_in, 1)
                            if tt:
                                pick_rows(tt - 1)
                        elif b < 3:
                            side = b - 1
                            src = posi[:, tt].rearrange("p h k -> p (h k)")
                            if side == 0:
                                step(dve.tensor_scalar(half_i[:], src, 4, None, ALU.logical_shift_right))
                            else:
                                step(dve.tensor_scalar(half_i[:], src, 15, None, ALU.bitwise_and))
                            step(dve.tensor_copy(half_f[:], half_i[:]))
                            step(tt_op(match[:], iota16, half_f[:].unsqueeze(2).to_broadcast([P, PICKS, TOPK]),
                                       ALU.is_equal))
                            m4 = match[:].rearrange("p (h k) a -> p h k a", h=PH)
                            t4 = topf[:, tt].rearrange("p (h s) a -> p h s a", s=2)[:, :, side, :]
                            step(tt_op(m4, m4, t4.unsqueeze(2).to_broadcast([P, PH, TOPK, TOPK]), ALU.mult))
                            if tt and side == 0:
                                dve.wait_ge(pick_mm, l * TT + tt)
                            step(dve.tensor_reduce(picked[:, side, :], match[:], AX_X, ALU.add))
                        else:
                            dve.wait_ge(gexp, l * TT + tt + 1)
                            if tt:
                                dve.wait_ge(picked_ready, l * TT + tt)
                            step(dve.tensor_reduce(gden[:, 0:8], best[:, tt], AX_X, ALU.add))
                            step(dve.reciprocal(gden[:, 0:8], gden[:, 0:8]))
                            tt_op(picked[:, 2, :].rearrange("p (h k) -> p h k", h=PH), best[:, tt],
                                  gden[:, 0:8].unsqueeze(2).to_broadcast([P, PH, TOPK]), ALU.mult
                                  ).then_inc(picked_ready, 1)
                pick_rows(TT - 1)
                dve.wait_ge(idx_ready, (l + 1) * TT)

                with dve.Fori(0, TT) as tt:
                    step.enter(tt, 1)
                    step(dve.tensor_copy(pick[:], idxT[:, bass.ds(tt, 1)].rearrange("p o a b -> p (o a) b")))
                    for n in range(32):
                        dve.wait_ge(hot_used, tt * 32 + (l * P + n + 1))
                        for q in range(4):
                            t = slice(4 * n + q, 4 * n + q + 1)
                            dve.tensor_scalar(hot_j[:, n % 2, q, :], iota, pick[:, 1, t], None, ALU.is_equal)
                            for r in range(2):
                                ins = dve.tensor_scalar(hot_i[:, n % 2, q, r, :], iota, pick[:, 0, t],
                                                        pick[:, 2 + r, t], ALU.is_equal, ALU.mult)
                        ins.then_inc(hot_ready, 1)
                    dve.wait_ge(hot_ready, tt * 32 + (l * P + 32))
                step.leave(TT)

                dve.wait_ge(hot_used, (l + 1) * P + 2)
                dve.memset(y[:], 0.0).then_inc(y_zero, 1)
                dve.wait_ge(y_zero, l + 1)

                def pair_lo(g, kk, s):
                    dve.wait_ge(w_hi_ready, g * 4 + (l * 64 + kk + 1))
                    tt_op(g_lo[:, s, 2 * kk:2 * kk + 2, :], a_in[:, kk], g_hi[:, s, 2 * kk:2 * kk + 2, :].bitcast(F32),
                          ALU.subtract).then_inc(w_ready, 1)

                def add_sums(g, dh):
                    dve.wait_ge(unit_used, g * 8 + (used(l, U_VE) + 4 * dh + 3))
                    dve.wait_ge(y_done, g * 2 + (l * 32 + dh + 1))
                    w = slice(dh * 512, dh * 512 + 512)
                    tt_op(y[:, :, w], y[:, :, w], ps[:, 4 * dh:4 * dh + 4, :], ALU.add).then_inc(y_done, 1)

                def sum_group(g, s, first=False, last=False):
                    for u in range(8):
                        if u == 0 and not first:
                            add_sums(g - 1, 1)
                        if u == 4:
                            add_sums(g, 0)
                        if u % 2 and not last:
                            pair_lo(g + 1, u // 2, 1 - s)

                for kk in range(4):
                    pair_lo(0, kk, 0)
                sum_group(0, 0, first=True)
                sum_group(1, 1)
                with dve.Fori(1, 7) as i:
                    sum_group(i * 2, 0)
                    sum_group(i * 2 + 1, 1)
                sum_group(14, 0)
                sum_group(15, 1, last=True)
                add_sums(15, 1)
                dve.wait_ge(y_done, (l + 1) * 32 + 2)
                step(tt_op(y[:], y[:], grow[:, 1, :].unsqueeze(1).to_broadcast([P, TT, D]), ALU.mult))
                for tt in range(TT):
                    ins = tt_op(x[:, tt, :], x[:, tt, :], y[:, tt, :], ALU.add)
                    if l == DEPTH - 1:
                        ins.then_inc(out_ready, 1)
                if l < DEPTH - 1:
                    ins.then_inc(x_ready, 1)
                    dve.wait_ge(x_ready, 2 * l + 2)
                    dve.sem_inc(small_free, 1)


_INS = ["stream", "x", "c", "cols", "rows", "w2", "sub", "rel", "onehot", "mask", "const"]


def lay_out(x, c, w_ada, b_ada, norm1_g, w_in, gla_gate_w2, gla_gate_b, gla_norm_g, swa_qnorm_g, swa_knorm_g,
            swa_sinks, rel_bias, w_up_a, w_up_b, w_out, norm2_g, peer_wq, peer_subkeys, peer_u, peer_v):
    f = np.float32

    def columns(w):
        n = w.shape[1] // P
        return w.reshape(KC, P, n, P).transpose(2, 1, 0, 3).reshape(n, P, 1024)

    def rows(w):
        k, n = w.shape[0] // 256, w.shape[1] // 512
        return w.reshape(k, 2, P, n, 512).transpose(3, 0, 2, 1, 4).reshape(n * k, P, 1024)

    def column(v):
        return v.reshape(-1, P).T

    stream = np.empty((DEPTH * N_STREAM, P, 1024), f)
    cols = np.empty((DEPTH, P, N_COLS), f)
    row = np.empty((DEPTH, P, DV + SH), f)
    at = np.cumsum([0, 512, 512, 1024, 16, 1024, 1024, 128, 128, 1024, 1024])
    for l in range(DEPTH):
        gq, gk, gv, lr, gr, sq, sk, sv, ga, gb = (w_in[l][:, at[j]:at[j + 1]] for j in range(10))
        lr = np.concatenate([lr, np.zeros((D, P - 16), f)], 1)
        sk2 = np.concatenate([sk[:, :HD], sk[:, :HD], sk[:, HD:], sk[:, HD:]], 1)
        units = [columns(w_ada[l]), columns(gq), columns(gk), columns(lr), rows(gv), columns(sq), columns(sk2),
                 columns(sv), rows(gr)]
        mix = [columns(w) for w in (ga, w_up_a[l], gb, w_up_b[l])]
        units.append(np.stack(mix, 1).reshape(4 * KC, P, 1024))
        units += [rows(w_out[l]), columns(peer_wq[l])]
        o = l * N_STREAM
        for u in units:
            stream[o:o + len(u)] = u
            o += len(u)
        stream[o:o + NK] = peer_u[l].reshape(NK, P, KC, P).transpose(0, 3, 2, 1).reshape(NK, P, 1024)
        stream[o + NK:o + 2 * NK] = peer_v[l].reshape(16, 4, 2, P, 2, 512).transpose(0, 4, 1, 3, 2, 5).reshape(
            NK, P, 1024)
        cols[l] = np.concatenate([column(norm1_g[l]), column(norm2_g[l]), column(b_ada[l]), column(gla_gate_b[l]),
                                  np.tile(swa_qnorm_g[l], 2)[:, None], np.tile(swa_knorm_g[l], 2)[:, None]], 1)
        row[l] = np.concatenate([gla_norm_g[l], swa_sinks[l]])[None, :]
    return {
        "stream": stream, "x": x.reshape(TT, P, D).transpose(1, 0, 2), "c": column(c), "cols": cols, "rows": row,
        "w2": gla_gate_w2, "sub": peer_subkeys.transpose(0, 3, 1, 2).reshape(DEPTH, P, 256), "rel": rel_bias,
        "onehot": bucket_onehot(), "mask": band_mask(), "const": constants(),
    }


def kernel(**inputs):
    import concourse.bacc as _bacc
    from concourse.bass_utils import run_bass_kernel_spmd as _run

    nc = _bacc.Bacc("TRN2", target_bir_lowering=False, num_devices=1)
    laid = lay_out(**{k: np.asarray(v) for k, v in inputs.items()})
    arrays, args = {}, []
    for name in _INS:
        a = np.ascontiguousarray(laid[name])
        arrays[f"in_{name}_dram"] = a
        args.append(nc.dram_tensor(f"in_{name}_dram", a.shape, mybir.dt.from_np(a.dtype), kind="ExternalInput").ap())
    args.append(nc.dram_tensor("out_0_dram", (SEQ, D), F32, kind="ExternalOutput").ap())
    trunk(nc, *args)
    r = _run(nc, [arrays], core_ids=[0])
    return r.results[0]["out_0_dram"].reshape(1, SEQ, D)
```

```python
from contextlib import ExitStack

import numpy as np

import concourse.bass as bass
from concourse import mybir

ALU = mybir.AluOpType
ACT = mybir.ActivationFunctionType
F32 = mybir.dt.float32
F32R = mybir.dt.float32r
U32 = mybir.dt.uint32
AX_X = mybir.AxisListType.X

P = 128
DEPTH, SEQ, D = 2, 512, 1024
TT = SEQ // P
KC = D // P
GH, DK, DV, CHUNK = 4, 128, 256, 64
SH, HD = 16, 64
EPS = 1e-6
NEG = -1.0e30
LOWEST = -3.0e38
GLA_TAU = 16.0
PH, NK, TOPK = 8, 128, 16
PICKS = PH * TOPK
GT = 64

N_ADA = 6 * KC
U_Q, U_K, U_LR, U_V, U_R, U_SQ, U_SK, U_SV, U_MIXA, U_MIXB = 0, 4, 8, 9, 17, 25, 33, 35, 36, 52
U_OUT, U_WQ, U_U = 68, 76, 92
U_VE = U_U + NK
N_SPLIT = U_VE + NK
N_ADA1 = 2 * KC
N_ADA2 = N_ADA - N_ADA1
RAW = 4
ORDER_OF = []
for _l in range(DEPTH):
    _o = [("w", m) for m in range(U_MIXA + 4)]
    for _h in range(SH):
        _o += [("a", N_ADA1 + 2 * _h), ("a", N_ADA1 + 2 * _h + 1)] + ([("w", U_MIXA + 4 + _h)] if _h < 14 else [])
    for _m in range(U_MIXB + 2, U_OUT + 2, 2):
        _o += [("w", _m), ("w", _m + 1)]
        if _l < DEPTH - 1:
            _o += [("a", _m - U_MIXB - 2), ("a", _m - U_MIXB - 1)]
    _o += [("w", m) for m in range(U_OUT + 2, U_WQ + 2)]
    ORDER_OF.append(_o + [("w", m) for m in range(U_WQ + 2, N_SPLIT)])
START = [sum(len(o) for o in ORDER_OF[:_l]) for _l in range(DEPTH + 1)]
PLACE = [{u: START[_l] + p for p, u in enumerate(ORDER_OF[_l])} for _l in range(DEPTH)]

COLUMN_UNITS = ([(m, "act") for m in range(U_Q, U_V)] + [(m, "act") for m in range(U_SQ, U_MIXA)]
                + [(m, "act" if m % 2 == 0 else "dve") for m in range(U_MIXA, U_OUT)]
                + [(m, "dve") for m in range(U_WQ, U_U)] + [(m, "act") for m in range(U_U, U_VE)])
ORDER = {m: n for n, (m, _) in enumerate(COLUMN_UNITS)}
DONE = {}
for _m, _e in COLUMN_UNITS:
    DONE[_m] = (_e, sum(1 for k, e in COLUMN_UNITS if e == _e and k <= _m))
ACT_DONE = sum(1 for _, e in COLUMN_UNITS if e == "act")
DVE_DONE = sum(1 for _, e in COLUMN_UNITS if e == "dve")

C_IDENT, C_IOTA, C_SCAN, C_CAUSAL, C_HEADS, C_ONES, N_CONST = 0, 128, 256, 768, 896, 1024, 1152
V_N1, V_N2, V_BADA, V_GB, V_QN, V_KN, N_COLS = 0, 8, 16, 64, 68, 69, 70


def constants():
    c = np.zeros((P, N_CONST), np.float32)
    i = np.arange(P)
    c[:, C_IDENT:C_IDENT + P] = np.eye(P)
    c[:, C_IOTA:C_IOTA + P] = i[None, :]
    c[:, C_SCAN:C_SCAN + SEQ] = (np.arange(SEQ) % CHUNK != 0)[None, :]
    same = i[:, None] // CHUNK == i[None, :] // CHUNK
    c[:, C_CAUSAL:C_CAUSAL + P] = same & (i[:, None] <= i[None, :])
    c[:, C_HEADS + 18] = (i < HD) / HD
    c[:, C_HEADS + 19] = (i >= HD) / HD
    c[:, C_ONES:C_ONES + P] = 1.0
    return c


def band_mask():
    dist = 255 - np.arange(384)
    return np.broadcast_to(np.where((dist >= 0) & (dist < 128), 0.0, NEG), (P, 384)).astype(np.float32)


def bucket_onehot():
    dist = 255 - np.arange(384)
    d = np.maximum(dist, 1).astype(np.float32)
    large = 16 + (np.log(d / 16) / np.log(128 / 16) * 16).astype(np.int32)
    bucket = np.where(dist < 16, dist, np.minimum(large, 31))
    out = np.zeros((32, 384), np.float32)
    for k in range(384):
        if 0 <= dist[k] < 128:
            out[bucket[k], k] = 1.0
    return out


class Chain:

    def __init__(self, eng, sem):
        self.eng, self.sem, self.n, self.off = eng, sem, 0, 0

    def __call__(self, ins):
        self.n += 1
        ins.then_inc(self.sem, 1)
        self.eng.wait_ge(self.sem, self.off + self.n)

    def enter(self, i, per):
        self.saved, self.per = self.n, per
        self.off, self.n = i * per + self.saved, 0

    def leave(self, count):
        assert self.n == self.per, self.n
        self.off, self.n = 0, self.saved + count * self.per


def trunk(nc, stream, x_in, c_in, cols_in, rows_in, w2_in, sub_in, rel_in, onehot_in, mask_in, const_in,
          out):
    band_d = nc.dram_tensor("band_bias", (SH, P * 384), F32, kind="Internal").ap()
    act_d = nc.dram_tensor("expert_act", (NK, P, SEQ), F32, kind="Internal").ap()
    gate_d = nc.dram_tensor("expert_gate", (SEQ // GT, P, NK, GT), F32, kind="Internal").ap()
    base = (nc.sbuf_base + 31) // 32 * 32

    def at(name, kb, shape, dt=F32):
        return nc.alloc_sbuf_tensor_at(name, shape, dt, offset=base + int(kb * 1024))

    x = at("x", 0, [P, TT, D])
    raw = at("raw", 16, [P, RAW, 1024])
    w_hi = at("w_hi", 32, [P, 2, 1024], F32R)
    w_lo = at("w_lo", 40, [P, 2, 1024], F32R)
    h_hi = at("h_hi", 48, [P, KC, SEQ], F32R)
    h_lo = at("h_lo", 64, [P, KC, SEQ], F32R)
    const = at("const", 80, [P, N_CONST])
    grow = at("grow", 84.5, [P, 2, D])
    cols = at("cols", 92.5, [P, DEPTH, N_COLS])
    rows = at("rows", 93.0625, [P, DV + SH])
    mod = at("mod", 94.125, [P, N_ADA])
    small = at("small", 94.3125, [P, 128])
    Z = 94.875
    ada_first = at("ada_first", Z + 32, [P, N_ADA1, 1024])
    v_g = at("v_g", Z + 0, [P, TT, D])
    r_g = at("r_g", Z + 16, [P, TT, D])
    qT_s = at("qT_s", Z + 32, [P, 8, SEQ])
    kT_s = at("kT_s", Z + 48, [P, 2, SEQ])
    vT_s = at("vT_s", Z + 52, [P, SEQ])
    v_s = at("v_s", Z + 54, [P, TT, P])
    q_g = at("q_g", Z + 56, [P, GH, SEQ])
    k_g = at("k_g", Z + 64, [P, GH, SEQ])
    kinv = at("kinv", Z + 72, [P, GH, SEQ])
    ktail = at("ktail", Z + 80, [P, GH, TT, P])
    tmp = at("tmp", Z + 88, [P, 5, SEQ])
    attnT = at("attnT", Z + 98, [P, 2, GH, P])
    state = at("state", Z + 102, [P, 2, GH, DV])
    w2 = at("w2", Z + 102, [16, SEQ])
    lrT = at("lrT", Z + 110, [16, SEQ])
    xn = at("xn", Z + 16, [P, TT, D])
    silu_first = at("silu_first", Z + 0, [P, D])
    silu_row = at("silu_row", Z + 92, [P, D])
    inv_rms = at("inv_rms", Z + 92, [20, SEQ])
    spread = at("spread", Z + 98, [20, 10 * P])
    hf = at("hf", Z + 88, [P, 4, SEQ])
    oa_hi = at("oa_hi", Z + 56, [P, KC, SEQ], F32R)
    oa_lo = at("oa_lo", Z + 72, [P, KC, SEQ], F32R)
    o_s = at("o_s", Z + 0, [P, TT, D])
    logit = at("logit", Z + 16, [P, 2, TT, 256])
    pT = at("pT", Z + 24, [P, 2, 8, P])
    bias_s = at("bias_s", Z + 88, [P, 4, 256])
    ob_hi = at("ob_hi", Z + 16, [P, KC, SEQ], F32R)
    ob_lo = at("ob_lo", Z + 32, [P, KC, SEQ], F32R)
    mixedT = at("mixedT", Z + 96, [P, KC, SEQ])
    sig_a = at("sig_a", 84.5, [P, 2, SEQ])
    sig = at("sig", Z + 0, [P, 4, SEQ])
    part = at("part", Z + 8, [P, 2, SEQ])
    diag = at("diag", Z + 48, [P, 16, P])
    xadd = at("xadd", Z + 56, [P, TT, SEQ])
    scores = at("scores", Z + 0, [P, TT, 16, P])
    gel = at("gel", Z + 32, [P, 2, SEQ])
    q_hi = at("q_hi", Z + 36, [P, 2, SEQ], F32R)
    q_lo = at("q_lo", Z + 40, [P, 2, SEQ], F32R)
    sub_raw = at("sub_raw", Z + 44, [P, 256])
    sub_hi = at("sub_hi", Z + 45, [P, 256], F32R)
    sub_lo = at("sub_lo", Z + 46, [P, 256], F32R)
    top = at("top", Z + 48, [P, TT, 16, TOPK])
    topf = at("topf", Z + 56, [P, TT, 16, TOPK])
    rest = at("rest", Z + 60, [P, TT, 256])
    cand = at("cand", Z + 64, [P, TT, 256])
    best = at("best", Z + 68, [P, TT, PH, TOPK])
    posi = at("posi", Z + 70, [P, TT, PH, TOPK], U32)
    half_i = at("half_i", Z + 72, [P, PICKS], U32)
    half_f = at("half_f", Z + 72.5, [P, PICKS])
    picked = at("picked", Z + 73, [P, 3, PICKS])
    gden = at("gden", Z + 74.5, [P, 16])
    match = at("match", Z + 76, [P, PH * TOPK, TOPK])
    pair_s = at("pair_s", Z + 84, [P, TT, 2, P])
    pair_t = at("pair_t", Z + 88, [P, TT, 2, TOPK])
    pair_i = at("pair_i", Z + 88.5, [P, TT, 2, TOPK], U32)
    pair_r = at("pair_r", Z + 89, [P, TT, 2, P])
    g_round = at("g_round", Z + 14, [P, TT, P], F32R)
    idxT = at("idxT", Z + 100, [P, TT, 4, P])
    gatebuf = at("gatebuf", Z + 36, [P, 2, NK, GT])
    hot_j = at("hot_j", Z + 0, [P, 2, 4, P], F32R)
    hot_i = at("hot_i", Z + 4, [P, 2, 4, 2, P], F32R)
    pick = at("pick", Z + 12, [P, 4, P])
    same_i = at("same_i", Z + 108, [P, 2, 4, P])
    y = at("y", Z + 0, [P, TT, D])
    g_hi = at("g_hi", Z + 16, [P, 2, 8, SEQ], F32R)
    g_lo = at("g_lo", Z + 48, [P, 2, 8, SEQ], F32R)
    a_in = at("a_in", Z + 80, [P, 4, 2, SEQ])
    g_in = at("g_in", Z + 96, [P, 4, SEQ // GT, 2, GT])
    rel = at("rel", Z + 96, [32, SH])
    onehot = at("onehot", Z + 96.5, [32, 384])
    mask_s = at("mask_s", Z + 98, [P, 384])
    band = at("band", 48, [P, SH, 384])

    ident = const[:, C_IDENT:C_IDENT + P]
    iota = const[:, C_IOTA:C_IOTA + P]

    with ExitStack() as ctx:
        ps = ctx.enter_context(nc.psum_tensor("ps", [P, 8, 512], F32))

        def sem(name):
            return ctx.enter_context(nc.semaphore(name))

        raw_loaded = [sem(f"raw_loaded{b}") for b in range(RAW)]
        ada_used, hi_ready, lo_ready, unit_used = sem("ada_used"), sem("hi_ready"), sem("lo_ready"), sem("unit_used")
        c_loaded, ada_first_loaded = sem("c_loaded"), [sem(f"ada_first_loaded{b}") for b in range(4)]
        col_act, col_dve, row_done = sem("col_act"), sem("col_dve"), sem("row_done")
        consts_loaded, x_loaded, params_loaded, small_free = (sem("consts_loaded"), sem("x_loaded"),
                                                              sem("params_loaded"), sem("small_free"))
        band_mm, band_out, band_stored, bias_free = sem("band_mm"), sem("band_out"), sem("band_stored"), sem("bias_free")
        bias_loaded = [sem(f"bias_loaded{b}") for b in range(4)]
        silu_ready, diag_ready, grow_mm = sem("silu_ready"), sem("diag_ready"), sem("grow_mm")
        sumsq, meansq, rstd, xn_ready, xT_mm, hf_ready, hhi_ready, h_ready = (
            sem("sumsq"), sem("meansq"), sem("rstd"), sem("xn_ready"), sem("xT_mm"), sem("hf_ready"),
            sem("hhi_ready"), sem("h_ready"))
        hf_act = sem("hf_act")
        x_ready, root_mm, spread_ready = sem("x_ready"), sem("root_mm"), sem("spread_ready")
        gate_mm, soft, decay, decay_exp, keys_ready, tail_mm, tail_ready = (
            sem("gate_mm"), sem("soft"), sem("decay"), sem("decay_exp"),
            sem("keys_ready"), sem("tail_mm"), sem("tail_ready"))
        attn_mm, attn_ready, upd_mm, state_ready, o_mm, o_sq, o_ms, o_rstd, o_done = (
            sem("attn_mm"), sem("attn_ready"), sem("upd_mm"), sem("state_ready"), sem("o_mm"), sem("o_sq"),
            sem("o_ms"), sem("o_rstd"), sem("o_done"))
        tr_mm, tr_hi, tr_done = sem("tr_mm"), sem("tr_hi"), sem("tr_done")
        sq_ready, sq_mm, sq_inv, sq_root, sqk_ready, vs_mm, vs_ready = (
            sem("sq_ready"), sem("sq_mm"), sem("sq_inv"), sem("sq_root"), sem("sqk_ready"), sem("vs_mm"), sem("vs_ready"))
        logit_mm, logit_ready, prob_ready, pT_mm, pT_ready, os_mm, os_ready = (
            sem("logit_mm"), sem("logit_ready"), sem("prob_ready"), sem("pT_mm"), sem("pT_ready"), sem("os_mm"),
            sem("os_ready"))
        mixed_sum, mixed_hi, mixed_ready, row_dve = sem("mixed_sum"), sem("mixed_hi"), sem("mixed_ready"), sem("row_dve")
        sub_loaded, subhi_ready, sub_ready, qhi_ready, score_mm, score_ready = (
            sem("sub_loaded"), sem("subhi_ready"), sem("sub_ready"), sem("qhi_ready"), sem("score_mm"), sem("score_ready"))
        gexp_in, gexp, picked_ready, pick_mm, ghi_ready, idx_ready = (
            sem("gexp_in"), sem("gexp"), sem("picked_ready"), sem("pick_mm"), sem("ghi_ready"), sem("idx_ready"))
        hot_ready, hot_used, gate_ready, gate_stored = (sem("hot_ready"), sem("hot_used"), sem("gate_ready"),
                                                        [sem("gate_stored0"), sem("gate_stored1")])
        gel_stored = [sem("gel_stored0"), sem("gel_stored1")]
        ag_loaded, w_prod, w_hi_ready, w_ready = ([sem(f"ag_loaded{b}") for b in range(4)], sem("w_prod"),
                                                  sem("w_hi_ready"), sem("w_ready"))
        y_done, out_ready, out_stored = sem("y_done"), sem("out_ready"), sem("out_stored")
        act_step, dve_step, fence = sem("act_step"), sem("dve_step"), sem("fence")
        y_zero, same_ready, w2_loaded = sem("y_zero"), sem("same_ready"), sem("w2_loaded")

        block = ctx.enter_context(nc.Block())

        def used(l, m):
            return l * N_SPLIT + m + 3

        def ada_count(l, n):
            return N_ADA1 + l * N_ADA + (n - N_ADA1 if n >= N_ADA1 else N_ADA2 + n) + 1

        @block.sync
        def _(sp):
            def load(place, b):
                sp.dma_start(raw[:, b, :], stream[bass.ds(place, 1)].rearrange("o p f -> p (o f)")
                             ).then_inc(raw_loaded[b], 16)

            def load_split(l, m, b):
                sp.wait_ge(lo_ready, m + (l * N_SPLIT - RAW + 1))
                load(m + (PLACE[l]["w", 0 + U_U] - U_U + N_ADA1), b)

            def load_listed(l, first, last):
                for p in range(first, last):
                    place = START[l] + p
                    if place >= RAW:
                        l0 = l if p >= RAW else l - 1
                        kind, k = ORDER_OF[l0][p - RAW]
                        if kind == "w":
                            sp.wait_ge(lo_ready, l0 * N_SPLIT + k + 1)
                        else:
                            sp.wait_ge(ada_used, ada_count(l0, k))
                    load(N_ADA1 + place, place % RAW)

            sp.dma_start(silu_first[:], c_in).then_inc(c_loaded, 16)
            sp.dma_start(rel[:], rel_in).then_inc(consts_loaded, 16)
            sp.dma_start(onehot[:], onehot_in).then_inc(consts_loaded, 16)
            sp.dma_start(mask_s[:], mask_in).then_inc(consts_loaded, 16)
            sp.dma_start(const[:], const_in).then_inc(consts_loaded, 16)
            sp.dma_start(cols[:], cols_in).then_inc(consts_loaded, 16)
            sp.dma_start(x[:], x_in).then_inc(x_loaded, 16)
            for n in range(N_ADA1):
                if n == 12:
                    for h in range(SH):
                        sp.wait_ge(band_out, h + 1)
                        sp.dma_start(band_d[h].rearrange("(p c) -> p c", p=P), band[:, h, :]).then_inc(band_stored, 16)
                sp.dma_start(ada_first[:, n, :], stream[n]).then_inc(ada_first_loaded[n // 4], 16)
            for half in range(2):
                sp.sem_inc(gate_stored[half], 16)
            for l in range(DEPTH):
                if l:
                    sp.wait_ge(small_free, l)
                sp.dma_start(rows[:], rows_in[l]).then_inc(params_loaded, 16)
                load_listed(l, 0, RAW)
                if l == 0:
                    sp.wait_ge(band_stored, 16 * SH)
                sp.dma_start(w2[:], w2_in[l]).then_inc(w2_loaded, 16)
                swa = U_MIXA + 4
                load_listed(l, RAW, swa + RAW)

                def load_bias(h):
                    sp.dma_start(bias_s[:, h % 4, :], band_d[h, P - 1:P - 1 + P * 383].rearrange(
                        "(q s) -> q s", s=383)[:, 0:256]).then_inc(bias_loaded[h % 4], 16)

                sp.wait_ge(bias_free, l * 13 + 1)
                sp.dma_start(silu_row[:], c_in).then_inc(c_loaded, 16)
                for h in range(4):
                    load_bias(h)
                at_head = swa + RAW
                for h in range(SH - 4):
                    load_listed(l, at_head, at_head + 3)
                    at_head += 3
                    sp.wait_ge(bias_free, l * 13 + h + 2)
                    load_bias(h + 4)
                queries = PLACE[l]["w", U_WQ + RAW] - START[l]
                load_listed(l, at_head, queries)
                sp.wait_ge(h_ready, (2 * l + 2) * KC)
                sp.dma_start(sub_raw[:], sub_in[l]).then_inc(sub_loaded, 16)
                load_listed(l, queries, queries + RAW)
                with sp.Fori(U_WQ // RAW + 2, U_VE // RAW - 2) as i:
                    for b in range(RAW):
                        load_split(l, i * RAW + b, b)
                def load_pair(pair, b):
                    src = bass.ds(pair * 2, 2)
                    sp.dma_start(a_in[:, b], act_d[src].rearrange("i j t -> j i t")).then_inc(ag_loaded[b], 16)
                    sp.dma_start(g_in[:, b].rearrange("p c i t -> p c (i t)"),
                                 gate_d[:, :, src].rearrange("c j i t -> j c (i t)")).then_inc(ag_loaded[b], 16)

                v0 = U_VE
                for n in range(v0 - 8, v0 - 4):
                    load_split(l, n, n % RAW)
                for half in range(2):
                    sp.wait_ge(gate_stored[half], 16 + (l + 1) * TT * 16)
                sp.wait_ge(y_zero, l + 1)
                sp.wait_ge(gel_stored[0], 16 * (l * (NK // 2) + 8) + 16)
                sp.wait_ge(gel_stored[1], 16 * (l * (NK // 2) + 8) + 16)
                for b in range(4):
                    load_pair(b, b)
                    load_split(l, v0 - 4 + b, b)
                for b in range(RAW):
                    load_split(l, v0 + b, b)
                for s in range(2):
                    sp.wait_ge(gel_stored[s], 16 + (l + 1) * (NK // 2) * 16)
                for b in range(4):
                    sp.wait_ge(w_ready, l * (NK // 2) + b + 1)
                    load_pair(4 + b, b)
                for b in range(RAW):
                    load_split(l, v0 + RAW + b, b)
                with sp.Fori(1, NK // 8 - 1) as g:
                    for k in range(2):
                        for b in range(RAW):
                            load_split(l, g * 8 + (v0 + k * RAW + b), b)
                        for b in (2 * k, 2 * k + 1):
                            sp.wait_ge(w_ready, g * 4 + (l * (NK // 2) + b + 1))
                            load_pair(g * 4 + (4 + b), b)
                for k in range(2):
                    for b in range(RAW):
                        load_split(l, N_SPLIT - 8 + k * RAW + b, b)
            for tt in range(TT):
                sp.wait_ge(out_ready, tt + 1)
                sp.dma_start(out[tt * P:(tt + 1) * P, :], x[:, tt, :]).then_inc(out_stored, 16)
            sp.wait_ge(out_stored, 16 * TT)

        @block.scalar
        def _(act):
            step = Chain(act, act_step)

            def copy(o, i):
                return act.activation(o, i, ACT.Copy)

            def split_at(l, m, r, s, b):
                act.wait_ge(raw_loaded[b], (r + 1) * 16)
                act.wait_ge(unit_used, used(l, m) - 2)
                copy(w_hi[:, s, :], raw[:, b, :]).then_inc(hi_ready, 1)

            def split_next(l, m):
                place = PLACE[l]["w", m]
                split_at(l, m, place // RAW, m % 2, place % RAW)

            def column_out(l, m, dst, func=ACT.Copy):
                act.activation(dst, ps[0:dst.shape[0], ORDER[m] % 2, :], func).then_inc(col_act, 1)

            def after_unit(l, m):
                act.wait_ge(unit_used, used(l, m))
                split_next(l, m + 2)
                if m < U_K:
                    column_out(l, m, q_g[:, m - U_Q, :])
                elif m < U_LR:
                    column_out(l, m, k_g[:, m - U_K, :])
                elif m == U_LR:
                    column_out(l, m, lrT[:])
                elif m in (U_V + 3, U_V + 7):
                    dh = (m - U_V) // 4
                    copy(v_g[:, :, dh * 512:dh * 512 + 512], ps[:, 4:8, :]).then_inc(row_done, 1)
                elif m in (U_R + 3, U_R + 7):
                    dh = (m - U_R) // 4
                    act.activation(r_g[:, :, dh * 512:dh * 512 + 512], ps[:, 4:8, :], ACT.Silu).then_inc(row_done, 1)
                elif m in range(U_SQ, U_SK):
                    column_out(l, m, qT_s[:, m - U_SQ, :])
                elif m in range(U_SK, U_SV):
                    column_out(l, m, kT_s[:, m - U_SK, :])
                elif m == U_SV:
                    column_out(l, m, vT_s[:])
                elif m in range(U_MIXA, U_MIXB, 2):
                    c = (m - U_MIXA) // 2
                    if c >= 2:
                        act.wait_ge(col_dve, l * DVE_DONE + c - 1)
                    column_out(l, m, sig_a[:, c % 2, :], ACT.Sigmoid)
                elif m in range(U_MIXB, U_OUT, 2):
                    c = (m - U_MIXB) // 2
                    if c >= 2:
                        act.wait_ge(col_dve, l * DVE_DONE + 8 + c - 1)
                    column_out(l, m, sig[:, c % 4, :], ACT.Sigmoid)

            def norm(k):
                if k == 0:
                    act.wait_ge(x_loaded, 16)
                for tt in range(TT):
                    if k:
                        act.wait_ge(x_ready, (k - 1) * TT + tt + 1)
                    act.activation(ps[:, 2:4, :], x[:, tt, :].rearrange("p (a b) -> p a b", a=2), ACT.Square,
                                   accum_out=small[:, tt:tt + 1]
                                   ).then_inc(sumsq, 1)
                    act.wait_ge(sumsq, k * TT + tt + 1)
                act.wait_ge(meansq, k + 1)
                act.activation(small[:, 4:8], small[:, 4:8], ACT.Sqrt).then_inc(rstd, 1)
                if k % 2 == 0:
                    split_next(k // 2, 0)
                    split_next(k // 2, 1)
                scale0, shift0 = (8, 0) if k % 2 == 0 else (32, 24)
                if k == 0:
                    act.wait_ge(band_stored, 16 * SH)

                def scaled(c):
                    act.wait_ge(xT_mm, k * KC + c + 1)
                    if c >= 4:
                        act.wait_ge(h_ready, k * KC + c - 3)
                    act.activation(hf[:, c % 4, :], ps[:, 4 + c % 4, :], ACT.Identity,
                                   scale=mod[:, scale0 + c:scale0 + c + 1], bias=mod[:, shift0 + c:shift0 + c + 1]
                                   ).then_inc(hf_act, 1)

                def upper(c):
                    if c % 2:
                        act.wait_ge(hf_act, k * 4 + c // 2 + 1)
                    else:
                        act.wait_ge(hf_ready, k * 4 + c // 2 + 1)
                    copy(h_hi[:, c, :], hf[:, c % 4, :]).then_inc(hhi_ready, 1)

                for c in range(0, KC, 2):
                    upper(c)
                    if c == 0:
                        scaled(1)
                    upper(c + 1)
                    if c + 3 < KC:
                        scaled(c + 3)

            def transposed_hi(dst, count):
                for c in range(KC):
                    act.wait_ge(tr_mm, count + c + 1)
                    copy(dst[:, c, :], ps[:, 4 + c % 4, :]).then_inc(tr_hi, 1)

            act.sem_inc(gel_stored[0], 16)
            act.sem_inc(gel_stored[1], 16)
            act.sem_inc(gate_ready, 2)
            act.wait_ge(consts_loaded, 80)
            act.wait_ge(c_loaded, 16)
            act.activation(silu_first[:], silu_first[:], ACT.Silu).then_inc(silu_ready, 1)

            for l in range(DEPTH):
                norm(2 * l)
                for m in range(U_R):
                    after_unit(l, m)
                for h in range(GH):
                    k = l * GH + h
                    gb = cols[:, l, V_GB + h:V_GB + h + 1]
                    act.wait_ge(gate_mm, k + 1)
                    if h:
                        act.wait_ge(keys_ready, k)
                    step(act.activation(tmp[:, 0, :], ps[:, 2 + h % 2, :], ACT.Abs, bias=gb))
                    step(act.activation(tmp[:, 0, :], tmp[:, 0, :], ACT.Exp, scale=-1.0))
                    act.activation(tmp[:, 0, :], tmp[:, 0, :], ACT.Ln, bias=1.0).then_inc(soft, 1)
                    act.wait_ge(decay, k + 1)
                    act.activation(tmp[:, 2, :], tmp[:, 1, :], ACT.Exp, scale=1.0 / GLA_TAU)
                    act.activation(tmp[:, 3, :], tmp[:, 1, :], ACT.Exp, scale=-1.0 / GLA_TAU)
                    for c in range(8):
                        act.activation(tmp[:, 4, c * 64:c * 64 + 64], tmp[:, 1, c * 64:c * 64 + 64], ACT.Exp,
                                       scale=-1.0 / GLA_TAU, bias=small[:, 8 + h * 8 + c:9 + h * 8 + c])
                    act.activation(small[:, 40 + h * 8:48 + h * 8], small[:, 8 + h * 8:16 + h * 8], ACT.Exp
                                   ).then_inc(decay_exp, 1)
                    after_unit(l, U_R + 2 * h)
                    after_unit(l, U_R + 2 * h + 1)
                    act.wait_ge(tail_mm, k + 1)
                    copy(ktail[:, h], ps[:, 0, :].rearrange("p (a b) -> p a b", a=TT)).then_inc(tail_ready, 1)
                for p in range(TT):
                    k = l * TT + p
                    for m in range(U_SQ + 3 * p, min(U_SQ + 3 * p + 3, U_MIXA)):
                        after_unit(l, m)
                    act.wait_ge(o_mm, k + 1)
                    for h in range(GH):
                        act.activation(tmp[:, h, 0:256], ps[:, 2 + h // 2, h % 2 * 256:h % 2 * 256 + 256],
                                       ACT.Square, accum_out=small[:, 72 + h:73 + h]).then_inc(o_sq, 1)
                    act.wait_ge(o_ms, k + 1)
                    act.activation(small[:, 76:80], small[:, 76:80], ACT.Sqrt).then_inc(o_rstd, 1)
                transposed_hi(oa_hi, l * 2 * KC)
                def square(t):
                    src = qT_s[:, t, :] if t < 8 else kT_s[:, t - 8, :]
                    if t >= 2:
                        act.wait_ge(sq_mm, l * 10 + t - 1)
                    act.activation(tmp[:, t % 2, :], src, ACT.Square).then_inc(sq_ready, 1)

                square(0)
                for t in range(1, 10):
                    square(t)
                after_unit(l, U_MIXA)
                act.wait_ge(sq_inv, l + 1)
                act.activation(inv_rms[:], inv_rms[:], ACT.Sqrt).then_inc(sq_root, 1)
                after_unit(l, U_MIXA + 1)

                def keep_pT(h):
                    k = l * SH + h
                    act.wait_ge(pT_mm, k + 1)
                    if h >= 2:
                        act.wait_ge(os_mm, k - 1)
                    copy(pT[:, h % 2], ps[:, 6:8, :].rearrange("p a (b c) -> p (a b) c", b=4)).then_inc(pT_ready, 1)

                act.wait_ge(c_loaded, 16 * (l + 2))
                act.activation(silu_row[:], silu_row[:], ACT.Silu).then_inc(silu_ready, 1)
                for h in range(SH):
                    s, w = h % 2, 80 + 12 * (h % 4)
                    act.wait_ge(logit_ready, l * SH + h + 1)
                    for b in range(TT):
                        act.activation(logit[:, s, b, :], logit[:, s, b, :], ACT.Exp,
                                       bias=small[:, w + b:w + b + 1], accum_out=small[:, w + 4 + b:w + 5 + b])
                    act.activation(small[:, w + 8:w + 12], small[:, w:w + 4], ACT.Exp,
                                   bias=rows[:, DV + h:DV + h + 1]).then_inc(prob_ready, 1)
                    if h:
                        keep_pT(h - 1)
                    if h == 0:
                        after_unit(l, U_MIXA + 2)
                    if h <= 12:
                        after_unit(l, U_MIXA + 3 + h)
                keep_pT(SH - 1)
                transposed_hi(ob_hi, l * 2 * KC + KC)
                for m in range(U_MIXB, U_OUT):
                    after_unit(l, m)
                for c in range(KC):
                    act.wait_ge(mixed_sum, l * KC + c + 1)
                    copy(h_hi[:, c, :], mixedT[:, c, :]).then_inc(mixed_hi, 1)
                for m in range(U_OUT, U_WQ):
                    after_unit(l, m)
                norm(2 * l + 1)
                act.wait_ge(sub_loaded, 16 * (l + 1))
                copy(sub_hi[:], sub_raw[:]).then_inc(subhi_ready, 1)

                def keep_scores(n):
                    act.wait_ge(score_mm, l * 16 + n + 1)
                    copy(scores[:, :, n, :], ps[:, 2 + n % 2, :].rearrange("p (a b) -> p a b", a=TT)
                         ).then_inc(score_ready, 1)

                for m in range(U_WQ, U_U):
                    n = m - U_WQ
                    act.wait_ge(unit_used, used(l, m))
                    split_next(l, m + 2)
                    if n >= 2:
                        act.wait_ge(score_mm, l * 16 + n - 1)
                    copy(q_hi[:, n % 2, :], ps[:, ORDER[m] % 2, :]).then_inc(qhi_ready, 1)
                    if n:
                        keep_scores(n - 1)
                keep_scores(15)

                def experts(i, n, first, extra=None):
                    for b in range(4):
                        mm = i * n + (U_U + first + b)
                        act.wait_ge(unit_used, used(l, mm))
                        split_at(l, mm + 2, i * (n // RAW) + (PLACE[l]["w", U_U] + first + b + 2) // RAW, b % 2, (b + 2) % RAW)
                        act.wait_ge(gel_stored[b % 2], i * (n * 8) + 16 * (l * NK + first + b - b % 2) // 2 + 16)
                        act.activation(gel[:, b % 2, :], ps[:, b % 2, :], ACT.Gelu_apprx_tanh).then_inc(col_act, 1)
                        if extra:
                            extra(b)
                        act.wait_ge(col_act, i * n + (l * ACT_DONE + DONE[U_U][1] + first + b))
                        act.dma_start(act_d[bass.ds(i * n + (first + b), 1)].rearrange("o j t -> j (o t)"),
                                      gel[:, b % 2, :]).then_inc(gel_stored[b % 2], 16)

                with act.Fori(0, 9) as i:
                    experts(i, 4, 0)
                for tt in range(TT):
                    def gate_exp(b):
                        if b == 1:
                            act.wait_ge(gexp_in, l * TT + tt + 1)
                            act.activation(best[:, tt], best[:, tt], ACT.Exp).then_inc(gexp, 1)

                    experts(0, 4, 36 + 4 * tt, gate_exp)
                    act.wait_ge(pick_mm, l * TT + tt + 1)
                    copy(idxT[:, tt, 0:2, :], ps[:, 4, 0:256].rearrange("p (a b) -> p a b", a=2))
                    copy(g_round[:, tt, :], ps[:, 4, 256:384]).then_inc(ghi_ready, 1)
                with act.Fori(0, TT) as tt:
                    def gates(k):
                        def extra(b):
                            for g in range(2):
                                n = (k * 4 + b) * 2 + g
                                half = n // 16
                                act.wait_ge(hot_used, tt * 32 + (l * P + n + 1 + 2))
                                if n % 16 == 0:
                                    act.wait_ge(gate_stored[half], tt * 16 + (l * TT * 16 + 16))
                                t = 4 * (n % 16)
                                copy(gatebuf[:, half, :, t:t + 4],
                                     ps[:, 4 + n % 2, :].rearrange("p (t i) -> p i t", t=4)).then_inc(gate_ready, 1)
                                if n % 16 == 15:
                                    act.wait_ge(gate_ready, tt * 32 + (l * P + n + 1 + 2))
                                    act.dma_start(gate_d[bass.ds(tt * 2 + half, 1)].rearrange("o j i t -> j (o i t)"),
                                                  gatebuf[:, half].rearrange("p i t -> p (i t)")
                                                  ).then_inc(gate_stored[half], 16)
                        return extra
                    for k in range(4):
                        experts(tt, 16, 52 + 4 * k, gates(k))
                def pair_hi(g, kk, s):
                    act.wait_ge(w_prod, g * 4 + (l * 64 + kk + 1))
                    copy(g_hi[:, s, 2 * kk:2 * kk + 2, :], a_in[:, kk]).then_inc(w_hi_ready, 1)

                def sum_group(g, s, last=False):
                    for u in range(8):
                        act.wait_ge(unit_used, g * 8 + used(l, U_VE + u))
                        if not (last and u > 5):
                            split_at(l, g * 8 + (U_VE + u + 2), g * 2 + (PLACE[l]["w", U_VE] + u + 2) // RAW, u % 2,
                                     (u + 2) % RAW)
                        if u % 2 and not last:
                            pair_hi(g + 1, u // 2, 1 - s)

                experts(0, 4, 116)
                experts(0, 4, 120)
                experts(0, 4, 124, lambda b: pair_hi(0, b, 0))
                with act.Fori(0, 7) as i:
                    sum_group(i * 2, 0)
                    sum_group(i * 2 + 1, 1)
                sum_group(14, 0)
                sum_group(15, 1, last=True)

        @block.gpsimd
        def _(pool):
            def split(m, b, s=None):
                s = b % 2 if s is None else s
                pool.wait_ge(hi_ready, m + 1)
                pool.tensor_tensor(w_lo[:, s, :], raw[:, b, :], w_hi[:, s, :].bitcast(F32), ALU.subtract
                                   ).then_inc(lo_ready, 1)

            def product(l, g, b):
                pool.wait_ge(ag_loaded[b], g * 32 + (l * 512 + 32))
                a4 = a_in[:, b].rearrange("p i (c t) -> p c i t", t=GT)
                pool.tensor_tensor(a4, a4, g_in[:, b], ALU.mult).then_inc(w_prod, 1)

            for l in range(DEPTH):
                v0 = l * N_SPLIT + U_VE
                for m in range(U_U):
                    split(l * N_SPLIT + m, PLACE[l]["w", m] % RAW, m % 2)
                with pool.Fori(U_U // RAW, U_VE // RAW - 1) as i:
                    for b in range(RAW):
                        split(i * RAW + (l * N_SPLIT + b), b)
                split(v0 - RAW, 0)
                for b in range(RAW - 1):
                    split(v0 - RAW + b + 1, b + 1)
                    product(l, 0, b)
                product(l, 0, RAW - 1)
                with pool.Fori(0, 15) as g:
                    for u in range(8):
                        split(g * 8 + (v0 + u), u % RAW)
                        if u % 2:
                            product(l, g + 1, u // 2)
                for u in range(8):
                    split(v0 + 120 + u, u % RAW)

        @block.tensor
        def _(pe):
            def column_unit(m, bank, s, mov_hi, mov_lo, width=P, arriving=None, before=0):
                o = ps[0:width, bank, :]
                for c in range(KC):
                    if arriving:
                        pe.wait_ge(arriving, before + c + 1)
                    w = slice(c * P, c * P + width)
                    pe.matmul(o, w_hi[:, s, w], mov_hi[:, c, :], start=c == 0, stop=False)
                    pe.matmul(o, w_lo[:, s, w], mov_hi[:, c, :], start=False, stop=False)
                    mm = pe.matmul(o, w_hi[:, s, w], mov_lo[:, c, :], start=False, stop=c == KC - 1)
                mm.then_inc(unit_used, 1)

            def row_unit(q, bank0, s, sta_hi, sta_lo):
                for kk in range(2):
                    w = slice(kk * 512, kk * 512 + 512)
                    for tt in range(TT):
                        t = slice(tt * P, tt * P + P)
                        first, last = q == 0 and kk == 0, q == 3 and kk == 1
                        o = ps[:, bank0 + tt, :]
                        pe.matmul(o, sta_hi[:, 2 * q + kk, t], w_hi[:, s, w], start=first, stop=False)
                        pe.matmul(o, sta_hi[:, 2 * q + kk, t], w_lo[:, s, w], start=False, stop=False)
                        mm = pe.matmul(o, sta_lo[:, 2 * q + kk, t], w_hi[:, s, w], start=False, stop=last)
                mm.then_inc(unit_used, 1)

            def column(l, m, mov_hi, mov_lo, width=P, arriving=None, before=0):
                pe.wait_ge(lo_ready, l * N_SPLIT + m + 1)
                n = ORDER[m]
                if n >= 2:
                    eng, count = DONE[COLUMN_UNITS[n - 2][0]]
                    if eng == "act":
                        pe.wait_ge(col_act, l * ACT_DONE + count)
                    else:
                        pe.wait_ge(col_dve, l * DVE_DONE + count)
                column_unit(m, n % 2, m % 2, mov_hi, mov_lo, width, arriving, before)

            def unit(l, m):
                if m in ORDER:
                    mov, ready = (h_hi, h_lo), {}
                    if m == U_Q:
                        ready = dict(arriving=h_ready, before=2 * l * KC)
                    if m in range(U_MIXA + 1, U_MIXB, 2):
                        mov = (oa_hi, oa_lo)
                        if m == U_MIXA + 1:
                            ready = dict(arriving=tr_done, before=l * 2 * KC)
                    elif m in range(U_MIXB + 1, U_OUT, 2):
                        mov = (ob_hi, ob_lo)
                        if m == U_MIXB + 1:
                            ready = dict(arriving=tr_done, before=l * 2 * KC + KC)
                    column(l, m, *mov, width=16 if m == U_LR else P, **ready)
                else:
                    j, q = (m - U_V) // 4, (m - U_V) % 4
                    pe.wait_ge(lo_ready, l * N_SPLIT + m + 1)
                    if q == 0 and j:
                        pe.wait_ge(row_done, l * 4 + j)
                    row_unit(q, 4, m % 2, h_hi, h_lo)

            def norm(k):
                for c in range(KC):
                    if c == 0:
                        pe.wait_ge(xn_ready, (k + 1) * TT)
                    if c >= 4:
                        pe.wait_ge(hf_act if c % 2 else hf_ready, k * 4 + (c - 4) // 2 + 1)
                    for tt in range(TT):
                        mm = pe.transpose(ps[:, 4 + c % 4, tt * P:(tt + 1) * P], xn[:, tt, c * P:(c + 1) * P], ident)
                    mm.then_inc(xT_mm, 1)

            def transposed(src, count):
                for c in range(KC):
                    if c >= 4:
                        pe.wait_ge(tr_done, count + c - 3)
                    for tt in range(TT):
                        mm = pe.transpose(ps[:, 4 + c % 4, tt * P:(tt + 1) * P], src[:, tt, c * P:(c + 1) * P], ident)
                    mm.then_inc(tr_mm, 1)

            pe.sem_inc(unit_used, 2)
            pe.sem_inc(hot_used, 2)
            pe.wait_ge(consts_loaded, 80)
            for h in range(SH):
                if h >= 2:
                    pe.wait_ge(band_out, h - 1)
                pe.matmul(ps[:, h % 2, 0:384], rel[:, h:h + 1].to_broadcast([32, P]), onehot[:], start=True, stop=True
                          ).then_inc(band_mm, 1)
            for l in range(DEPTH):
                norm(2 * l)
                for m in range(U_R):
                    unit(l, m)
                pe.wait_ge(w2_loaded, (l + 1) * 16)
                pe.wait_ge(col_act, l * ACT_DONE + DONE[U_LR][1])

                def gate(h):
                    if h >= 2:
                        pe.wait_ge(decay, l * GH + h - 1)
                    pe.matmul(ps[:, 2 + h % 2, :], w2[:, h * P:(h + 1) * P], lrT[:], start=True, stop=True
                              ).then_inc(gate_mm, 1)

                gate(0)
                for h in range(GH):
                    k = l * GH + h
                    if h < GH - 1:
                        gate(h + 1)
                    unit(l, U_R + 2 * h)
                    unit(l, U_R + 2 * h + 1)
                    pe.wait_ge(keys_ready, k + 1)
                    if h:
                        pe.wait_ge(tail_ready, k)
                    for p in range(TT):
                        mm = pe.transpose(ps[:, 0, p * P:(p + 1) * P], k_g[:, h, p * P:(p + 1) * P], ident)
                    mm.then_inc(tail_mm, 1)
                pe.wait_ge(row_done, l * 4 + 4)
                for p in range(TT):
                    k = l * TT + p
                    if p:
                        pe.wait_ge(attn_ready, k)
                    for h in range(GH):
                        mm = pe.matmul(ps[:, 6, h * P:(h + 1) * P], kinv[:, h, p * P:(p + 1) * P],
                                       q_g[:, h, p * P:(p + 1) * P], start=True, stop=True)
                    mm.then_inc(attn_mm, 1)
                    if p == 0:
                        pe.wait_ge(tail_ready, l * GH + GH)
                    for e in range(2):
                        c = 2 * p + e
                        if e:
                            unit(l, U_SQ + 3 * p)
                        if c == 7:
                            break
                        if c:
                            pe.wait_ge(state_ready, l * 7 + c)
                        r = slice(64 * e, 64 * e + 64)
                        for h in range(GH):
                            mm = pe.matmul(ps[:, 4 + h // 2, h % 2 * 256:h % 2 * 256 + 256], ktail[r, h, p, :],
                                           v_g[r, p, h * DV:(h + 1) * DV], start=True, stop=True)
                        mm.then_inc(upd_mm, 1)
                    for m in range(U_SQ + 3 * p + 1, min(U_SQ + 3 * p + 3, U_MIXA)):
                        unit(l, m)
                    pe.wait_ge(attn_ready, k + 1)
                    pe.wait_ge(state_ready, l * 7 + 2 * p + 1)
                    if p:
                        pe.wait_ge(o_done, k)
                    for h in range(GH):
                        o = ps[:, 2 + h // 2, h % 2 * 256:h % 2 * 256 + 256]
                        t0 = p * P
                        pe.matmul(o, attnT[:, p % 2, h, :], v_g[:, p, h * DV:(h + 1) * DV], start=True, stop=False,
                                  skip_group_check=True)
                        if p:
                            pe.matmul(o[0:64], q_g[:, h, t0:t0 + 64], state[:, 0, h, :], start=False, stop=False,
                                      skip_group_check=True)
                        mm = pe.matmul(o[64:128], q_g[:, h, t0 + 64:t0 + 128], state[:, 1, h, :], start=False, stop=True,
                                       skip_group_check=True)
                    mm.then_inc(o_mm, 1)
                unit(l, U_MIXA)
                pe.wait_ge(o_done, (l + 1) * TT)
                transposed(r_g, l * 2 * KC)
                for t in range(10):
                    pe.wait_ge(sq_ready, l * 10 + t + 1)
                    w = C_HEADS + 18 - 2 * t
                    pe.matmul(ps[0:20, 2, :], const[:, w:w + 20], tmp[:, t % 2, :], start=t == 0, stop=t == 9
                              ).then_inc(sq_mm, 1)
                for b in range(TT):
                    mm = pe.transpose(ps[:, 3, b * P:(b + 1) * P], vT_s[:, b * P:(b + 1) * P], ident)
                mm.then_inc(vs_mm, 1)
                unit(l, U_MIXA + 1)
                pe.wait_ge(sq_root, l + 1)
                pe.wait_ge(spread_ready, l + 1)
                pe.wait_ge(vs_ready, l + 1)
                for t in range(10):
                    if t >= 2:
                        pe.wait_ge(sqk_ready, l * 10 + t - 1)
                    pe.matmul(ps[:, 2 + t % 2, :], spread[:, t * P:t * P + P], inv_rms[:], start=True, stop=True
                              ).then_inc(root_mm, 1)
                pe.wait_ge(sqk_ready, (l + 1) * 10)

                def logits(h):
                    if h:
                        pe.wait_ge(logit_ready, l * SH + h)
                    r = slice(HD * (h % 2), HD * (h % 2) + HD)
                    kv = h // 8
                    for b in range(TT):
                        o = ps[:, 4 + b // 2, b % 2 * 256:b % 2 * 256 + 256]
                        q = qT_s[r, h // 2, b * P:(b + 1) * P]
                        if b == 0:
                            mm = pe.matmul(o[:, 128:256], q, kT_s[r, kv, 0:P], start=True, stop=True)
                        else:
                            mm = pe.matmul(o, q, kT_s[r, kv, (b - 1) * P:(b + 1) * P], start=True, stop=True)
                    mm.then_inc(logit_mm, 1)

                def probs(h):
                    pe.wait_ge(prob_ready, l * SH + h + 1)
                    if h:
                        pe.wait_ge(pT_ready, l * SH + h)
                    for j in range(1, 8):
                        mm = pe.transpose(ps[:, 6 + j // 4, j % 4 * P:j % 4 * P + P],
                                          logit[:, h % 2, j // 2, j % 2 * P:j % 2 * P + P], ident)
                    mm.then_inc(pT_mm, 1)

                def values(h):
                    pe.wait_ge(pT_ready, l * SH + h + 1)
                    if h:
                        pe.wait_ge(os_ready, l * SH + h)
                    kv = slice(h // 8 * HD, h // 8 * HD + HD)
                    for b in range(TT):
                        o = ps[:, 3, b * HD:b * HD + HD]
                        if b:
                            pe.matmul(o, pT[:, h % 2, 2 * b, :], v_s[:, b - 1, kv], start=True, stop=False)
                        mm = pe.matmul(o, pT[:, h % 2, 2 * b + 1, :], v_s[:, b, kv], start=b == 0, stop=True)
                    mm.then_inc(os_mm, 1)

                logits(0)
                unit(l, U_MIXA + 2)
                unit(l, U_MIXA + 3)
                for h in range(SH):
                    if h < SH - 1:
                        logits(h + 1)
                    probs(h)
                    if h < 12:
                        unit(l, U_MIXA + 4 + h)
                    if h:
                        values(h - 1)
                unit(l, U_MIXB)
                values(SH - 1)
                pe.wait_ge(os_ready, (l + 1) * SH)
                transposed(o_s, l * 2 * KC + KC)
                for m in range(U_MIXB + 1, U_OUT):
                    unit(l, m)
                    if m == U_MIXB + 1:
                        pe.wait_ge(diag_ready, l + 1)
                        for j in range(16):
                            mm = pe.matmul(ps[:, 4 + j // 4, j % 4 * P:j % 4 * P + P], const[:, C_ONES:C_ONES + P],
                                           diag[:, j, :], start=True, stop=True)
                        mm.then_inc(grow_mm, 1)
                for m in range(U_OUT, U_WQ):
                    q, j = (m - U_OUT) % 4, (m - U_OUT) // 4
                    pe.wait_ge(lo_ready, l * N_SPLIT + m + 1)
                    if j == 0:
                        pe.wait_ge(mixed_ready, l * KC + 2 * q + 2)
                    elif q == 0:
                        pe.wait_ge(row_dve, l + 1)
                    row_unit(q, 4, m % 2, h_hi, h_lo)
                norm(2 * l + 1)

                def score(n):
                    pe.wait_ge(col_dve, l * DVE_DONE + 16 + n + 1)
                    if n == 0:
                        pe.wait_ge(sub_ready, l + 1)
                    if n >= 2:
                        pe.wait_ge(score_ready, l * 16 + n - 1)
                    k = slice(n % 2 * P, n % 2 * P + P)
                    for tt in range(TT):
                        t = slice(tt * P, tt * P + P)
                        o = ps[:, 2 + n % 2, t]
                        pe.matmul(o, q_hi[:, n % 2, t], sub_hi[:, k], start=True, stop=False)
                        pe.matmul(o, q_hi[:, n % 2, t], sub_lo[:, k], start=False, stop=False)
                        mm = pe.matmul(o, q_lo[:, n % 2, t], sub_hi[:, k], start=False, stop=True)
                    mm.then_inc(score_mm, 1)

                for n in range(16):
                    column(l, U_WQ + n, h_hi, h_lo, arriving=None if n else h_ready, before=(2 * l + 1) * KC)
                    if n:
                        score(n - 1)
                score(15)

                def experts(i, n, first, extra=None):
                    for b in range(4):
                        e = i * n + (first + b)
                        pe.wait_ge(lo_ready, e + (l * N_SPLIT + U_U + 1))
                        pe.wait_ge(col_act, e + (l * ACT_DONE + DONE[U_U][1] - 2))
                        column_unit(None, b % 2, b % 2, h_hi, h_lo)
                        if extra:
                            extra(b)

                with pe.Fori(0, 9) as i:
                    experts(i, 4, 0)
                for tt in range(TT):
                    experts(0, 4, 36 + 4 * tt)
                    pe.wait_ge(picked_ready, l * TT + tt + 1)
                    if tt:
                        pe.wait_ge(idx_ready, l * TT + tt)
                    for r in range(3):
                        mm = pe.transpose(ps[:, 4, r * P:(r + 1) * P], picked[:, r, :], ident)
                    mm.then_inc(pick_mm, 1)
                pe.wait_ge(idx_ready, (l + 1) * TT)
                with pe.Fori(0, TT) as tt:
                    def gates(k):
                        def extra(b):
                            for g in range(2):
                                n = (k * 4 + b) * 2 + g
                                pe.wait_ge(hot_ready, tt * 32 + (l * P + n + 1))
                                pe.wait_ge(gate_ready, tt * 32 + (l * P + n + 1))
                                for q in range(4):
                                    o = ps[:, 4 + n % 2, q * P:(q + 1) * P]
                                    pe.matmul(o, hot_j[:, n % 2, q, :], hot_i[:, n % 2, q, 0, :], start=True, stop=False)
                                    mm = pe.matmul(o, hot_j[:, n % 2, q, :], hot_i[:, n % 2, q, 1, :], start=False,
                                                   stop=True)
                                mm.then_inc(hot_used, 1)
                        return extra
                    for k in range(4):
                        experts(tt, 16, 52 + 4 * k, gates(k))

                for k in range(3):
                    experts(0, 4, 116 + 4 * k)
                pe.wait_ge(col_act, (l + 1) * ACT_DONE)

                def sum_group(g, s):
                    for u in range(8):
                        if u < 4:
                            pe.wait_ge(w_ready, g * 4 + (l * 64 + u + 1))
                        pe.wait_ge(lo_ready, g * 8 + (l * N_SPLIT + U_VE + u + 1))
                        if u % 4 == 0:
                            pe.wait_ge(y_done, g * 2 + (l * 32 + u // 4 + 1))
                        row_unit(u % 4, u // 4 * 4, u % 2, g_hi[:, s], g_lo[:, s])

                with pe.Fori(0, 8) as i:
                    sum_group(i * 2, 0)
                    sum_group(i * 2 + 1, 1)

        @block.vector
        def _(dve):
            step = Chain(dve, dve_step)
            tt_op = dve.tensor_tensor

            def settle(ins):
                step(ins)
                dve.sem_inc(fence, 1)

            def norm(k, before_scale=None):
                scale0, shift0 = (8, 0) if k % 2 == 0 else (32, 24)
                dve.wait_ge(sumsq, (k + 1) * TT)
                step(dve.tensor_scalar(small[:, 4:8], small[:, 0:4], 1.0 / D, EPS, ALU.mult, ALU.add))
                dve.reciprocal(small[:, 4:8], small[:, 4:8]).then_inc(meansq, 1)
                dve.wait_ge(rstd, k + 1)
                for tt in range(TT):
                    dve.tensor_scalar(xn[:, tt, :], x[:, tt, :], small[:, 4 + tt:5 + tt], None, ALU.mult
                                      ).then_inc(xn_ready, 1)
                if before_scale:
                    before_scale()
                for c in range(0, KC + 2, 2):
                    if c < KC:
                        dve.wait_ge(xT_mm, k * KC + c + 1)
                        if c >= 4:
                            dve.wait_ge(h_ready, k * KC + c - 3)
                        dve.tensor_scalar(hf[:, c % 4, :], ps[:, 4 + c % 4, :], mod[:, scale0 + c:scale0 + c + 1],
                                          mod[:, shift0 + c:shift0 + c + 1], ALU.mult, ALU.add).then_inc(hf_ready, 1)
                    if c:
                        norm_lo(k, c - 2)
                        norm_lo(k, c - 1)

            def norm_lo(k, c):
                dve.wait_ge(hhi_ready, k * KC + c + 1)
                tt_op(h_lo[:, c, :], hf[:, c % 4, :], h_hi[:, c, :].bitcast(F32), ALU.subtract).then_inc(h_ready, 1)

            def transposed_lo(dst, hi, count):
                for c in range(KC):
                    dve.wait_ge(tr_hi, count + c + 1)
                    tt_op(dst[:, c, :], ps[:, 4 + c % 4, :], hi[:, c, :].bitcast(F32), ALU.subtract).then_inc(tr_done, 1)

            dve.sem_inc(y_done, 2)
            dve.wait_ge(consts_loaded, 80)
            for h in range(SH):
                dve.wait_ge(band_mm, h + 1)
                tt_op(band[:, h, :], ps[:, h % 2, 0:384], mask_s[:], ALU.add).then_inc(band_out, 1)


            def modulation_unit(w, row, n):
                dve.tensor_tensor_reduce(w, w, row[:], 1.0, 0.0, ALU.mult, ALU.add, accum_out=mod[:, n:n + 1]
                                         ).then_inc(ada_used, 1)

            def streamed_modulation(l, n):
                place = PLACE[l]["a", n]
                dve.wait_ge(raw_loaded[place % RAW], 16 * (place // RAW + 1))
                modulation_unit(raw[:, place % RAW, :], silu_row, n)

            def first_modulation():
                dve.wait_ge(silu_ready, 1)
                for n in range(N_ADA1):
                    if n % 4 == 0:
                        dve.wait_ge(ada_first_loaded[n // 4], 64)
                    modulation_unit(ada_first[:, n, :], silu_first, n)
                modulation(0, 0, N_ADA1, N_ADA1)

            def modulation(l, first, count, ready):
                dve.wait_ge(ada_used, ready)
                w = slice(first, first + count)
                step(tt_op(mod[:, w], mod[:, w], cols[:, l, V_BADA + first:V_BADA + first + count], ALU.add))
                a, v = (8, V_N1) if first == 0 else (32, V_N2)
                step(dve.scalar_tensor_tensor(out=mod[:, a:a + 8], in0=mod[:, a:a + 8], scalar=1.0,
                                              in1=cols[:, l, v:v + 8], op0=ALU.add, op1=ALU.mult))

            def decay_of(l, h):
                k = l * GH + h
                dve.wait_ge(soft, k + 1)
                step(dve.tensor_scalar(tmp[:, 1, :], ps[:, 2 + h % 2, :], cols[:, l, V_GB + h:V_GB + h + 1], 0.0,
                                       ALU.add, ALU.min))
                step(tt_op(tmp[:, 2, :], tmp[:, 1, :], tmp[:, 0, :], ALU.subtract))
                step(dve.tensor_tensor_scan(tmp[:, 1, :], const[:, C_SCAN:C_SCAN + SEQ], tmp[:, 2, :], 0.0,
                                            ALU.mult, ALU.add))
                dve.tensor_scalar(small[:, 8 + h * 8:16 + h * 8], tmp[:, 1, CHUNK - 1:SEQ:CHUNK], 1.0 / GLA_TAU, None,
                                  ALU.mult).then_inc(decay, 1)
                dve.wait_ge(decay_exp, k + 1)
                dve.scalar_tensor_tensor(out=q_g[:, h, :], in0=q_g[:, h, :], scalar=DK ** -0.5, in1=tmp[:, 2, :],
                                         op0=ALU.mult, op1=ALU.mult)
                tt_op(kinv[:, h, :], k_g[:, h, :], tmp[:, 3, :], ALU.mult)
                tt_op(k_g[:, h, :], k_g[:, h, :], tmp[:, 4, :], ALU.mult).then_inc(keys_ready, 1)
                dve.wait_ge(keys_ready, k + 1)

            def gated_a(l, c):
                m = U_MIXA + 2 * c + 1
                dve.wait_ge(unit_used, used(l, m))
                dve.wait_ge(col_act, l * ACT_DONE + DONE[m - 1][1])
                tt_op(mixedT[:, c, :], ps[:, ORDER[m] % 2, :], sig_a[:, c % 2, :], ALU.mult).then_inc(col_dve, 1)

            for l in range(DEPTH):
                dve.tensor_scalar(cols[:, l, V_QN:V_QN + 1], cols[:, l, V_QN:V_QN + 1], HD ** -0.5, None, ALU.mult)
                norm(2 * l, first_modulation if l == 0 else None)
                for h in range(GH):
                    decay_of(l, h)
                dve.wait_ge(params_loaded, (l + 1) * 16)
                dve.wait_ge(row_done, l * 4 + 4)
                r16 = r_g[:].rearrange("p t (h v) -> p (t h) v", h=GH)
                step(tt_op(r16, r16, rows[:, 0:DV].unsqueeze(1).to_broadcast([P, 16, DV]), ALU.mult))
                step(dve.memset(attnT[:], 0.0))
                mask = const[:, C_CAUSAL:C_CAUSAL + P].bitcast(U32).unsqueeze(1).to_broadcast([P, GH, P])

                def update(c):
                    dve.wait_ge(upd_mm, l * 7 + c + 1)
                    if c == 1:
                        dve.wait_ge(o_mm, l * TT + 1)
                    elif c > 1:
                        dve.wait_ge(o_mm, l * TT + (c + 1) // 2)
                    for h in range(GH):
                        u = ps[:, 4 + h // 2, h % 2 * 256:h % 2 * 256 + 256]
                        new = state[:, (c + 1) % 2, h, :]
                        if c == 0:
                            ins = dve.tensor_copy(new, u)
                        else:
                            ins = dve.scalar_tensor_tensor(out=new, in0=state[:, c % 2, h, :],
                                                           scalar=small[:, 40 + h * 8 + c:41 + h * 8 + c], in1=u,
                                                           op0=ALU.mult, op1=ALU.add)
                    ins.then_inc(state_ready, 1)
                    dve.wait_ge(state_ready, l * 7 + c + 1)

                for p in range(TT):
                    k = l * TT + p
                    dve.wait_ge(attn_mm, k + 1)
                    if p >= 2:
                        dve.wait_ge(o_mm, k - 1)
                    dve.copy_predicated(attnT[:, p % 2], mask, ps[:, 6, :].rearrange("p (a b) -> p a b", a=GH)
                                        ).then_inc(attn_ready, 1)
                    update(2 * p)
                    dve.wait_ge(o_sq, l * 16 + 4 * (p + 1))
                    if p:
                        dve.wait_ge(o_done, k)
                    step(dve.tensor_scalar(small[:, 76:80], small[:, 72:76], 1.0 / DV, EPS, ALU.mult, ALU.add))
                    dve.reciprocal(small[:, 76:80], small[:, 76:80]).then_inc(o_ms, 1)
                    if p < TT - 1:
                        update(2 * p + 1)
                    dve.wait_ge(o_rstd, k + 1)
                    for h in range(GH):
                        r = r_g[:, p, h * DV:(h + 1) * DV]
                        ins = dve.scalar_tensor_tensor(out=r, in0=ps[:, 2 + h // 2, h % 2 * 256:h % 2 * 256 + 256],
                                                       scalar=small[:, 76 + h:77 + h], in1=r, op0=ALU.mult, op1=ALU.mult)
                    ins.then_inc(o_done, 1)
                transposed_lo(oa_lo, oa_hi, l * 2 * KC)
                dve.tensor_copy(spread[:].rearrange("k (a b) -> k a b", b=HD),
                                ident[0:20, 0:20].unsqueeze(2).to_broadcast([20, 20, HD])).then_inc(spread_ready, 1)
                dve.wait_ge(vs_mm, l + 1)
                dve.tensor_copy(v_s[:], ps[:, 3, :].rearrange("p (a b) -> p a b", a=TT)).then_inc(vs_ready, 1)
                dve.wait_ge(sq_mm, (l + 1) * 10)
                step(dve.tensor_scalar(inv_rms[:], ps[0:20, 2, :], EPS, None, ALU.add))
                dve.reciprocal(inv_rms[:], inv_rms[:]).then_inc(sq_inv, 1)
                for t in range(10):
                    src = qT_s[:, t, :] if t < 8 else kT_s[:, t - 8, :]
                    g = cols[:, l, V_QN:V_QN + 1] if t < 8 else cols[:, l, V_KN:V_KN + 1]
                    dve.wait_ge(root_mm, l * 10 + t + 1)
                    dve.scalar_tensor_tensor(out=src, in0=src, scalar=g, in1=ps[:, 2 + t % 2, :], op0=ALU.mult,
                                             op1=ALU.mult).then_inc(sqk_ready, 1)
                gated_a(l, 0)
                dve.wait_ge(sqk_ready, (l + 1) * 10)
                dve.sem_inc(bias_free, 1)

                def finish(h):
                    w = 80 + 12 * (h % 4)
                    den = small[:, w + 4:w + 8]
                    dve.wait_ge(prob_ready, l * SH + h + 1)
                    step(tt_op(den, den, small[:, w + 8:w + 12], ALU.add))
                    step(dve.reciprocal(den, den))
                    dve.wait_ge(os_mm, l * SH + h + 1)
                    tt_op(o_s[:, :, h * HD:(h + 1) * HD], ps[:, 3, 0:256].rearrange("p (a b) -> p a b", a=TT),
                          den.unsqueeze(2).to_broadcast([P, TT, HD]), ALU.mult).then_inc(os_ready, 1)

                for h in range(SH):
                    k, s = l * SH + h, h % 2
                    lp = ps[:, 4:6, :].rearrange("p a (b c) -> p (a b) c", b=2)
                    dve.wait_ge(logit_mm, k + 1)
                    if h >= 2:
                        dve.wait_ge(pT_mm, k - 1)
                    dve.wait_ge(bias_loaded[h % 4], 16 * (l * 4 + h // 4 + 1))
                    dve.memset(logit[:, s, 0, 0:P], NEG)
                    tt_op(logit[:, s, 0, P:2 * P], lp[:, 0, P:2 * P], bias_s[:, h % 4, P:2 * P], ALU.add)
                    step(tt_op(logit[:, s, 1:4, :], lp[:, 1:4, :], bias_s[:, h % 4, :].unsqueeze(1).to_broadcast([P, 3, 256]),
                               ALU.add))
                    if h < SH - 4:
                        dve.sem_inc(bias_free, 1)
                    mx = small[:, 80 + 12 * (h % 4):84 + 12 * (h % 4)]
                    step(dve.tensor_reduce(mx, logit[:, s], AX_X, ALU.max))
                    dve.tensor_scalar(mx, mx, rows[:, DV + h:DV + h + 1], -1.0, ALU.max, ALU.mult).then_inc(logit_ready, 1)
                    if h == 0:
                        dve.wait_ge(silu_ready, l + 2)
                    streamed_modulation(l, N_ADA1 + 2 * h)
                    streamed_modulation(l, N_ADA1 + 2 * h + 1)
                    if h in range(0, 13, 2):
                        gated_a(l, h // 2 + 1)
                    if h >= 2:
                        finish(h - 2)
                finish(SH - 2)
                finish(SH - 1)
                transposed_lo(ob_lo, ob_hi, l * 2 * KC + KC)
                modulation(l, N_ADA1, N_ADA2, ada_count(l, N_ADA - 1))
                for j in range(16):
                    g = (16 if j < 8 else 40) + j % 8
                    ins = dve.tensor_scalar(diag[:, j, :], ident, mod[:, g:g + 1], None, ALU.mult)
                ins.then_inc(diag_ready, 1)
                for c in range(KC):
                    m = U_MIXB + 2 * c + 1
                    dve.wait_ge(unit_used, used(l, m))
                    dve.wait_ge(col_act, l * ACT_DONE + DONE[m - 1][1])
                    if c >= 2:
                        dve.wait_ge(mixed_sum, l * KC + c - 1)
                    tt_op(part[:, c % 2, :], ps[:, ORDER[m] % 2, :], sig[:, c % 4, :], ALU.mult).then_inc(col_dve, 1)
                    dve.wait_ge(col_dve, l * DVE_DONE + DONE[m][1])
                    tt_op(mixedT[:, c, :], mixedT[:, c, :], part[:, c % 2, :], ALU.add).then_inc(mixed_sum, 1)
                    if c == 0:
                        dve.wait_ge(grow_mm, l + 1)
                        step(dve.tensor_copy(grow[:], ps[:, 4:8, :].rearrange("p (a b) c -> p a (b c)", a=2)))
                    if l < DEPTH - 1:
                        streamed_modulation(l, 2 * c)
                        streamed_modulation(l, 2 * c + 1)
                for c in range(KC):
                    dve.wait_ge(mixed_hi, l * KC + c + 1)
                    tt_op(h_lo[:, c, :], mixedT[:, c, :], h_hi[:, c, :].bitcast(F32), ALU.subtract).then_inc(mixed_ready, 1)
                for m in range(U_OUT, U_WQ):
                    if (m - U_OUT) % 4 == 3:
                        dh = (m - U_OUT) // 4
                        dve.wait_ge(unit_used, used(l, m))
                        w = slice(dh * 512, dh * 512 + 512)
                        if dh == 0:
                            tt_op(xadd[:], ps[:, 4:8, :], grow[:, 0, w].unsqueeze(1).to_broadcast([P, TT, 512]),
                                  ALU.mult).then_inc(row_dve, 1)
                            dve.wait_ge(row_dve, l + 1)
                            step(tt_op(x[:, :, w], x[:, :, w], xadd[:], ALU.add))
                        else:
                            for tt in range(TT):
                                step(tt_op(xadd[:, tt, :], ps[:, 4 + tt, :], grow[:, 0, w], ALU.mult))
                                tt_op(x[:, tt, w], x[:, tt, w], xadd[:, tt, :], ALU.add).then_inc(x_ready, 1)
                dve.wait_ge(x_ready, (2 * l + 1) * TT)
                norm(2 * l + 1)
                if l < DEPTH - 1:
                    modulation(l + 1, 0, N_ADA1, ada_count(l, N_ADA1 - 1))
                dve.wait_ge(subhi_ready, l + 1)
                tt_op(sub_lo[:], sub_raw[:], sub_hi[:].bitcast(F32), ALU.subtract).then_inc(sub_ready, 1)
                for m in range(U_WQ, U_U):
                    n = m - U_WQ
                    dve.wait_ge(qhi_ready, l * 16 + n + 1)
                    tt_op(q_lo[:, n % 2, :], ps[:, ORDER[m] % 2, :], q_hi[:, n % 2, :].bitcast(F32), ALU.subtract
                          ).then_inc(col_dve, 1)

                def top16(vals, rest_v, tops, idx, count):
                    for j in range(count):
                        ins = dve.max(tops(j)[:, 0:8], vals(j))
                    settle(ins)
                    for j in range(count):
                        ins = dve.match_replace(rest_v(j), tops(j)[:, 0:8], vals(j), LOWEST)
                    settle(ins)
                    for j in range(count):
                        ins = dve.max(tops(j)[:, 8:16], rest_v(j))
                        dve.max_index(idx(j)[:, 0:8], tops(j)[:, 0:8], vals(j))
                    settle(ins)
                    for j in range(count):
                        ins = dve.max_index(idx(j)[:, 8:16], tops(j)[:, 8:16], rest_v(j))
                    settle(ins)

                dve.wait_ge(score_ready, (l + 1) * 16)
                with dve.Fori(0, PH) as i:
                    step.enter(i, 11)
                    settle(dve.tensor_copy(pair_s[:], scores[:, :, bass.ds(i * 2, 2), :]))
                    for side in range(2):
                        top16(lambda j: pair_s[:, j, side, :], lambda j: pair_r[:, j, side, :],
                              lambda j: pair_t[:, j, side, :], lambda j: pair_i[:, j, side, :], TT)
                    step(dve.tensor_copy(top[:, :, bass.ds(i * 2, 2), :], pair_t[:]))
                    step(dve.tensor_copy(topf[:, :, bass.ds(i * 2, 2), :], pair_i[:]))
                    step.leave(PH)
                with dve.Fori(0, PH) as i:
                    step.enter(i, 6)
                    s1 = top[:, :, bass.ds(i * 2, 1), :].rearrange("p t o a -> p t (o a)")
                    s2 = top[:, :, bass.ds(i * 2 + 1, 1), :].rearrange("p t o a -> p t (o a)")
                    for tt in range(TT):
                        ins = tt_op(cand[:, tt, :].rearrange("p (a b) -> p a b", a=TOPK),
                                    s1[:, tt, :].unsqueeze(2).to_broadcast([P, TOPK, TOPK]),
                                    s2[:, tt, :].unsqueeze(1).to_broadcast([P, TOPK, TOPK]), ALU.add)
                    settle(ins)
                    top16(lambda j: cand[:, j, :], lambda j: rest[:, j, :], lambda j: pair_t[:, j, 0, :],
                          lambda j: pair_i[:, j, 0, :], TT)
                    dve.tensor_copy(best[:, :, bass.ds(i, 1), :], pair_t[:, :, 0:1, :])
                    step(dve.tensor_copy(posi[:, :, bass.ds(i, 1), :], pair_i[:, :, 0:1, :]))
                    step.leave(PH)

                def pick_rows(tt):
                    dve.wait_ge(ghi_ready, l * TT + tt + 1)
                    dve.tensor_copy(idxT[:, tt, 2, :], g_round[:, tt, :].bitcast(F32))
                    tt_op(idxT[:, tt, 3, :], ps[:, 4, 256:384], g_round[:, tt, :].bitcast(F32), ALU.subtract
                          ).then_inc(idx_ready, 1)

                iota16 = const[:, C_IOTA:C_IOTA + TOPK].unsqueeze(1).to_broadcast([P, PICKS, TOPK])
                for tt in range(TT):
                    for b in range(4):
                        if b == 0:
                            step(dve.tensor_copy(gden[:, 8:16], best[:, tt, :, 0]))
                            tt_op(best[:, tt], best[:, tt], gden[:, 8:16].unsqueeze(2).to_broadcast([P, PH, TOPK]),
                                  ALU.subtract).then_inc(gexp_in, 1)
                            if tt:
                                pick_rows(tt - 1)
                        elif b < 3:
                            side = b - 1
                            src = posi[:, tt].rearrange("p h k -> p (h k)")
                            if side == 0:
                                step(dve.tensor_scalar(half_i[:], src, 4, None, ALU.logical_shift_right))
                            else:
                                step(dve.tensor_scalar(half_i[:], src, 15, None, ALU.bitwise_and))
                            step(dve.tensor_copy(half_f[:], half_i[:]))
                            step(tt_op(match[:], iota16, half_f[:].unsqueeze(2).to_broadcast([P, PICKS, TOPK]),
                                       ALU.is_equal))
                            m4 = match[:].rearrange("p (h k) a -> p h k a", h=PH)
                            t4 = topf[:, tt].rearrange("p (h s) a -> p h s a", s=2)[:, :, side, :]
                            step(tt_op(m4, m4, t4.unsqueeze(2).to_broadcast([P, PH, TOPK, TOPK]), ALU.mult))
                            if tt and side == 0:
                                dve.wait_ge(pick_mm, l * TT + tt)
                            step(dve.tensor_reduce(picked[:, side, :], match[:], AX_X, ALU.add))
                        else:
                            dve.wait_ge(gexp, l * TT + tt + 1)
                            if tt:
                                dve.wait_ge(picked_ready, l * TT + tt)
                            step(dve.tensor_reduce(gden[:, 0:8], best[:, tt], AX_X, ALU.add))
                            step(dve.reciprocal(gden[:, 0:8], gden[:, 0:8]))
                            tt_op(picked[:, 2, :].rearrange("p (h k) -> p h k", h=PH), best[:, tt],
                                  gden[:, 0:8].unsqueeze(2).to_broadcast([P, PH, TOPK]), ALU.mult
                                  ).then_inc(picked_ready, 1)
                pick_rows(TT - 1)
                dve.wait_ge(idx_ready, (l + 1) * TT)

                iota4 = iota.unsqueeze(1).to_broadcast([P, 4, P])
                with dve.Fori(0, TT) as tt:
                    step.enter(tt, 1)
                    step(dve.tensor_copy(pick[:], idxT[:, bass.ds(tt, 1)].rearrange("p o a b -> p (o a) b")))
                    def row(n, r):
                        return pick[:, r, 4 * n:4 * n + 4].unsqueeze(2).to_broadcast([P, 4, P])

                    def match_i(n):
                        tt_op(same_i[:, n % 2], iota4, row(n, 0), ALU.is_equal).then_inc(same_ready, 1)

                    match_i(0)
                    for n in range(32):
                        dve.wait_ge(hot_used, tt * 32 + (l * P + n + 1))
                        tt_op(hot_j[:, n % 2], iota4, row(n, 1), ALU.is_equal)
                        if n < 31:
                            if n:
                                dve.wait_ge(hot_ready, tt * 32 + (l * P + n))
                            match_i(n + 1)
                        dve.wait_ge(same_ready, tt * 32 + (l * P + n + 1))
                        tt_op(hot_i[:, n % 2, :, 0, :], same_i[:, n % 2], row(n, 2), ALU.mult)
                        tt_op(hot_i[:, n % 2, :, 1, :], same_i[:, n % 2], row(n, 3), ALU.mult).then_inc(hot_ready, 1)
                    dve.wait_ge(hot_ready, tt * 32 + (l * P + 32))
                step.leave(TT)

                dve.wait_ge(hot_used, (l + 1) * P + 2)
                dve.memset(y[:], 0.0).then_inc(y_zero, 1)
                dve.wait_ge(y_zero, l + 1)

                def pair_lo(g, kk, s):
                    dve.wait_ge(w_hi_ready, g * 4 + (l * 64 + kk + 1))
                    tt_op(g_lo[:, s, 2 * kk:2 * kk + 2, :], a_in[:, kk], g_hi[:, s, 2 * kk:2 * kk + 2, :].bitcast(F32),
                          ALU.subtract).then_inc(w_ready, 1)

                def add_sums(g, dh):
                    dve.wait_ge(unit_used, g * 8 + (used(l, U_VE) + 4 * dh + 3))
                    dve.wait_ge(y_done, g * 2 + (l * 32 + dh + 1))
                    w = slice(dh * 512, dh * 512 + 512)
                    tt_op(y[:, :, w], y[:, :, w], ps[:, 4 * dh:4 * dh + 4, :], ALU.add).then_inc(y_done, 1)

                def sum_group(g, s, first=False, last=False):
                    for u in range(8):
                        if u == 0 and not first:
                            add_sums(g - 1, 1)
                        if u == 4:
                            add_sums(g, 0)
                            if last:
                                dve.wait_ge(y_done, (l + 1) * 32 + 1)
                                step(tt_op(y[:, :, 0:512], y[:, :, 0:512],
                                           grow[:, 1, 0:512].unsqueeze(1).to_broadcast([P, TT, 512]), ALU.mult))
                                step(tt_op(x[:, :, 0:512], x[:, :, 0:512], y[:, :, 0:512], ALU.add))
                        if u % 2 and not last:
                            pair_lo(g + 1, u // 2, 1 - s)

                for kk in range(4):
                    pair_lo(0, kk, 0)
                sum_group(0, 0, first=True)
                sum_group(1, 1)
                with dve.Fori(1, 7) as i:
                    sum_group(i * 2, 0)
                    sum_group(i * 2 + 1, 1)
                sum_group(14, 0)
                sum_group(15, 1, last=True)
                add_sums(15, 1)
                dve.wait_ge(y_done, (l + 1) * 32 + 2)
                for tt in range(TT):
                    step(tt_op(y[:, tt, 512:], y[:, tt, 512:], grow[:, 1, 512:], ALU.mult))
                    tt_op(x[:, tt, 512:], x[:, tt, 512:], y[:, tt, 512:], ALU.add
                          ).then_inc(x_ready if l < DEPTH - 1 else out_ready, 1)
                if l < DEPTH - 1:
                    dve.wait_ge(x_ready, (2 * l + 2) * TT)
                    dve.sem_inc(small_free, 1)


_INS = ["stream", "x", "c", "cols", "rows", "w2", "sub", "rel", "onehot", "mask", "const"]


def lay_out(x, c, w_ada, b_ada, norm1_g, w_in, gla_gate_w2, gla_gate_b, gla_norm_g, swa_qnorm_g, swa_knorm_g,
            swa_sinks, rel_bias, w_up_a, w_up_b, w_out, norm2_g, peer_wq, peer_subkeys, peer_u, peer_v):
    f = np.float32

    def columns(w):
        n = w.shape[1] // P
        return w.reshape(KC, P, n, P).transpose(2, 1, 0, 3).reshape(n, P, 1024)

    def rows(w):
        k, n = w.shape[0] // 256, w.shape[1] // 512
        return w.reshape(k, 2, P, n, 512).transpose(3, 0, 2, 1, 4).reshape(n * k, P, 1024)

    def column(v):
        return v.reshape(-1, P).T

    stream = np.empty((N_ADA1 + START[DEPTH], P, 1024), f)
    cols = np.empty((P, DEPTH, N_COLS), f)
    ada_units = w_ada.reshape(DEPTH, D, N_ADA, P).transpose(0, 2, 3, 1)
    stream[0:N_ADA1] = ada_units[0, 0:N_ADA1]
    row = np.empty((DEPTH, P, DV + SH), f)
    at = np.cumsum([0, 512, 512, 1024, 16, 1024, 1024, 128, 128, 1024, 1024])
    for l in range(DEPTH):
        gq, gk, gv, lr, gr, sq, sk, sv, ga, gb = (w_in[l][:, at[j]:at[j + 1]] for j in range(10))
        lr = np.concatenate([lr, np.zeros((D, P - 16), f)], 1)
        sk2 = np.concatenate([sk[:, :HD], sk[:, :HD], sk[:, HD:], sk[:, HD:]], 1)
        units = [columns(gq), columns(gk), columns(lr), rows(gv), rows(gr), columns(sq), columns(sk2), columns(sv)]
        for gate, up in ((ga, w_up_a[l]), (gb, w_up_b[l])):
            units.append(np.stack([columns(gate), columns(up)], 1).reshape(2 * KC, P, 1024))
        units += [rows(w_out[l]), columns(peer_wq[l])]
        split = np.concatenate(units)
        for (kind, k), place in PLACE[l].items():
            if kind == "a":
                stream[N_ADA1 + place] = ada_units[l if k >= N_ADA1 else l + 1, k]
            elif k < U_U:
                stream[N_ADA1 + place] = split[k]
        o = N_ADA1 + PLACE[l]["w", U_U]
        stream[o:o + NK] = peer_u[l].reshape(NK, P, KC, P).transpose(0, 3, 2, 1).reshape(NK, P, 1024)
        stream[o + NK:o + 2 * NK] = peer_v[l].reshape(16, 4, 2, P, 2, 512).transpose(0, 4, 1, 3, 2, 5).reshape(
            NK, P, 1024)
        cols[:, l] = np.concatenate([column(norm1_g[l]), column(norm2_g[l]), column(b_ada[l]), column(gla_gate_b[l]),
                                  np.tile(swa_qnorm_g[l], 2)[:, None], np.tile(swa_knorm_g[l], 2)[:, None]], 1)
        row[l] = np.concatenate([gla_norm_g[l], swa_sinks[l]])[None, :]
    return {
        "stream": stream, "x": x.reshape(TT, P, D).transpose(1, 0, 2),
        "c": np.broadcast_to(c.reshape(1, D), (P, D)), "cols": cols, "rows": row,
        "w2": gla_gate_w2, "sub": peer_subkeys.transpose(0, 3, 1, 2).reshape(DEPTH, P, 256), "rel": rel_bias,
        "onehot": bucket_onehot(), "mask": band_mask(), "const": constants(),
    }


def kernel(**inputs):
    import concourse.bacc as _bacc
    from concourse.bass_utils import run_bass_kernel_spmd as _run

    nc = _bacc.Bacc("TRN2", target_bir_lowering=False, num_devices=1)
    laid = lay_out(**{k: np.asarray(v) for k, v in inputs.items()})
    arrays, args = {}, []
    for name in _INS:
        a = np.ascontiguousarray(laid[name])
        arrays[f"in_{name}_dram"] = a
        args.append(nc.dram_tensor(f"in_{name}_dram", a.shape, mybir.dt.from_np(a.dtype), kind="ExternalInput").ap())
    args.append(nc.dram_tensor("out_0_dram", (SEQ, D), F32, kind="ExternalOutput").ap())
    trunk(nc, *args)
    r = _run(nc, [arrays], core_ids=[0])
    return r.results[0]["out_0_dram"].reshape(1, SEQ, D)
```
